# Optimizing a Trainium2 kernel written in Bass

```python
import jax, jax.numpy as jnp
from jax import lax
import numpy as np

D_MODEL = 1024
BATCH = 1
SEQ = 512
DEPTH = 1

SB_HEADS = 8
SB_HEAD_DIM = 64
SB_WIDTH = SB_HEADS * SB_HEAD_DIM
SB_BLOCK = 128

GLA_HEADS = 4
GLA_DK = 64
GLA_DV = 128
GLA_KW = GLA_HEADS * GLA_DK
GLA_VW = GLA_HEADS * GLA_DV
GLA_RANK = 16
GLA_TAU = 16.0
GLA_CHUNK = 64

D_FF = 2816
CONV_WIDTH = 3

EPS = 1e-6

IN_SIZES = (SB_WIDTH, SB_WIDTH, SB_WIDTH,
            GLA_KW, GLA_KW, GLA_VW, GLA_VW,
            GLA_RANK,
            D_MODEL, D_MODEL)
IN_TOTAL = sum(IN_SIZES)


def rms_norm(x, g):
    xf = x.astype(jnp.float32)
    xf = xf * lax.rsqrt(jnp.mean(xf * xf, axis=-1, keepdims=True) + EPS)
    return xf.astype(x.dtype) * g

def to_heads(t, n_heads):
    b, s, _ = t.shape
    return t.reshape(b, s, n_heads, -1).transpose(0, 2, 1, 3)

def from_heads(t):
    b, h, s, d = t.shape
    return t.transpose(0, 2, 1, 3).reshape(b, s, h * d)

def stick_breaking_attention(q, k, v):
    s_len, dh = q.shape[2], q.shape[3]
    scale = dh ** -0.5
    outs = []
    for i0 in range(0, s_len, SB_BLOCK):
        end = i0 + SB_BLOCK
        qb = q[:, :, i0:end]
        kb = k[:, :, :end]
        vb = v[:, :, :end]
        z = jnp.einsum('bhqd,bhkd->bhqk', qb, kb).astype(jnp.float32) * scale
        t_idx = i0 + jnp.arange(SB_BLOCK)[:, None]
        s_idx = jnp.arange(end)[None, :]
        strict = s_idx < t_idx
        log_keep = jnp.where(strict, jax.nn.log_sigmoid(-z), 0.0)
        tail = lax.cumsum(log_keep, axis=3, reverse=True) - log_keep
        log_w = jax.nn.log_sigmoid(z) + tail
        w = jnp.where(strict, jnp.exp(log_w), 0.0)
        outs.append(jnp.einsum('bhqk,bhkd->bhqd', w.astype(v.dtype), vb))
    return jnp.concatenate(outs, axis=2)

def gla_chunked(q, k, v, log_a):
    b, h, s_len, dk = q.shape
    dv = v.shape[-1]
    c = GLA_CHUNK
    n = s_len // c
    qf = q.astype(jnp.float32).reshape(b, h, n, c, dk)
    kf = k.astype(jnp.float32).reshape(b, h, n, c, dk)
    vf = v.astype(jnp.float32).reshape(b, h, n, c, dv)
    cum = jnp.cumsum(log_a.reshape(b, h, n, c, dk), axis=3)
    cum_last = cum[:, :, :, -1:]
    q_dec = qf * jnp.exp(cum)
    k_inv = kf * jnp.exp(-cum)
    k_to_end = kf * jnp.exp(cum_last - cum)
    att = jnp.einsum('bhnck,bhnsk->bhncs', q_dec, k_inv)
    causal = jnp.tril(jnp.ones((c, c), dtype=bool))
    att = jnp.where(causal, att, 0.0)
    o_intra = jnp.einsum('bhncs,bhnsv->bhncv', att, vf)
    d_state = jnp.einsum('bhnck,bhncv->bhnkv', k_to_end, vf)
    chunk_decay = jnp.exp(cum_last[:, :, :, 0])

    def step(state, inp):
        dec, ds = inp
        return dec[..., None] * state + ds, state

    init = jnp.zeros((b, h, dk, dv), jnp.float32)
    _, states_before = lax.scan(step, init,
                                (jnp.moveaxis(chunk_decay, 2, 0), jnp.moveaxis(d_state, 2, 0)))
    states_before = jnp.moveaxis(states_before, 0, 2)
    o_inter = jnp.einsum('bhnck,bhnkv->bhncv', q_dec, states_before)
    return (o_intra + o_inter).reshape(b, h, s_len, dv)

def mixing_sublayer(xn, w_in, b_gate, w_alpha_up, b_alpha, gla_norm_g,
                    w_branch_sb, w_branch_gla, w_out):
    proj = xn @ w_in
    offsets = np.cumsum(IN_SIZES)[:-1].tolist()
    (sb_q, sb_k, sb_v, g_q, g_k, g_v, g_r, g_a,
     gate_sb, gate_gla) = jnp.split(proj, offsets, axis=-1)

    o_sb = stick_breaking_attention(to_heads(sb_q, SB_HEADS),
                                    to_heads(sb_k, SB_HEADS),
                                    to_heads(sb_v, SB_HEADS))
    o_sb = from_heads(o_sb)

    a_pre = (g_a @ w_alpha_up + b_alpha).astype(jnp.float32)
    log_a = jax.nn.log_sigmoid(a_pre) / GLA_TAU
    o_gla = gla_chunked(to_heads(g_q, GLA_HEADS) * (GLA_DK ** -0.5),
                        to_heads(g_k, GLA_HEADS),
                        to_heads(g_v, GLA_HEADS),
                        to_heads(log_a, GLA_HEADS))
    o_gla = o_gla * lax.rsqrt(jnp.mean(o_gla * o_gla, axis=-1, keepdims=True) + EPS)
    o_gla = from_heads(o_gla).astype(xn.dtype) * gla_norm_g * jax.nn.silu(g_r)

    y = (jax.nn.sigmoid(gate_sb + b_gate[0]) * (o_sb @ w_branch_sb)
         + jax.nn.sigmoid(gate_gla + b_gate[1]) * (o_gla @ w_branch_gla))
    return y @ w_out

def causal_depthwise_conv(u, w, bias):
    k_w = w.shape[0]
    s_len = u.shape[1]
    up = jnp.pad(u, ((0, 0), (k_w - 1, 0), (0, 0)))
    out = bias
    for i in range(k_w):
        out = out + up[:, i:i + s_len] * w[i]
    return out

def conv_ffn(hn, w_ffn_in, conv_w, conv_b, w_ffn_out):
    u = hn @ w_ffn_in
    a, g = jnp.split(u, 2, axis=-1)
    a = causal_depthwise_conv(a, conv_w, conv_b)
    return (jax.nn.gelu(a) * g) @ w_ffn_out

def first_inputs(seed: int = 0) -> dict:
    key = jax.random.key(seed)
    ks = jax.random.split(key, 16)
    f32 = jnp.float32

    def nrm(k, shape, scale):
        return jax.random.normal(k, shape, f32) * scale

    return {
        "x": jax.random.normal(ks[0], (BATCH, SEQ, D_MODEL), f32),
        "norm_mix_g": 1.0 + nrm(ks[1], (DEPTH, D_MODEL), 0.02),
        "w_in": nrm(ks[2], (DEPTH, D_MODEL, IN_TOTAL), D_MODEL ** -0.5),
        "b_gate": nrm(ks[3], (DEPTH, 2, D_MODEL), 0.02),
        "w_alpha_up": nrm(ks[4], (DEPTH, GLA_RANK, GLA_KW), GLA_RANK ** -0.5),
        "b_alpha": nrm(ks[5], (DEPTH, GLA_KW), 0.1),
        "gla_norm_g": 1.0 + nrm(ks[6], (DEPTH, GLA_VW), 0.02),
        "w_branch_sb": nrm(ks[7], (DEPTH, SB_WIDTH, D_MODEL), SB_WIDTH ** -0.5),
        "w_branch_gla": nrm(ks[8], (DEPTH, GLA_VW, D_MODEL), GLA_VW ** -0.5),
        "w_out": nrm(ks[9], (DEPTH, D_MODEL, D_MODEL), D_MODEL ** -0.5),
        "norm_ffn_g": 1.0 + nrm(ks[10], (DEPTH, D_MODEL), 0.02),
        "w_ffn_in": nrm(ks[11], (DEPTH, D_MODEL, 2 * D_FF), D_MODEL ** -0.5),
        "conv_w": nrm(ks[12], (DEPTH, CONV_WIDTH, D_FF), CONV_WIDTH ** -0.5),
        "conv_b": nrm(ks[13], (DEPTH, D_FF), 0.01),
        "w_ffn_out": nrm(ks[14], (DEPTH, D_FF, D_MODEL), D_FF ** -0.5),
        "norm_final_g": 1.0 + nrm(ks[15], (D_MODEL,), 0.02),
    }

def first_block(x, norm_mix_g, w_in, b_gate, w_alpha_up, b_alpha, gla_norm_g,
              w_branch_sb, w_branch_gla, w_out, norm_ffn_g, w_ffn_in, conv_w,
              conv_b, w_ffn_out, norm_final_g):
    h = x
    for i in range(DEPTH):
        xn = rms_norm(h, norm_mix_g[i])
        h = h + mixing_sublayer(xn, w_in[i], b_gate[i], w_alpha_up[i], b_alpha[i],
                                gla_norm_g[i], w_branch_sb[i], w_branch_gla[i], w_out[i])
        hn = rms_norm(h, norm_ffn_g[i])
        h = h + conv_ffn(hn, w_ffn_in[i], conv_w[i], conv_b[i], w_ffn_out[i])
    return rms_norm(h, norm_final_g)


DEPTH_2 = 2

GRID_W = 64

POOL_WINDOWS = (2, 4, 8, 16)
N_POOL_GROUPS = 4
POOL_GROUP_DIM = D_MODEL // 8
POOL_DIM = N_POOL_GROUPS * POOL_GROUP_DIM

ATT_HEADS = 8
ATT_KV_HEADS = 2
ATT_HEAD_DIM = D_MODEL // 16
ATT_Q_DIM = ATT_HEADS * ATT_HEAD_DIM
ATT_KV_DIM = ATT_KV_HEADS * ATT_HEAD_DIM
Q_BLOCK = 128
ROPE_THETA = 10000.0

EVEN_IN_DIM = POOL_DIM + ATT_Q_DIM + 2 * ATT_KV_DIM
EVEN_MIX_DIM = POOL_DIM + ATT_Q_DIM

MLSTM_HEADS = 8
MLSTM_QK_DIM = D_MODEL // 16
MLSTM_V_DIM = D_MODEL // 8
MLSTM_QK_WIDTH = MLSTM_HEADS * MLSTM_QK_DIM
MLSTM_V_WIDTH = MLSTM_HEADS * MLSTM_V_DIM
N_GATES = 4 * MLSTM_HEADS
ODD_IN_DIM = 2 * MLSTM_QK_WIDTH + 2 * MLSTM_V_WIDTH + N_GATES
CONV_K = 5
CHUNK = 128

FFN_HIDDEN = -(-8 * D_MODEL // (3 * 256)) * 256


def rms_norm_2(x):
    x32 = x.astype(jnp.float32)
    y = x32 * lax.rsqrt(jnp.mean(x32 * x32, axis=-1, keepdims=True) + EPS)
    return y.astype(x.dtype)

def modulate(h, shift, scale):
    return h * (1.0 + scale[:, None, :]) + shift[:, None, :]

def grid_rope(seq_len):
    rows = seq_len // GRID_W
    row = jnp.repeat(jnp.arange(rows), GRID_W).astype(jnp.float32)
    col = jnp.tile(jnp.arange(GRID_W), rows).astype(jnp.float32)
    n_freq = ATT_HEAD_DIM // 4
    inv_freq = ROPE_THETA ** (-jnp.arange(n_freq, dtype=jnp.float32) / n_freq)
    ang = jnp.concatenate([row[:, None] * inv_freq, col[:, None] * inv_freq], axis=-1)
    return jnp.cos(ang), jnp.sin(ang)

def apply_rope(x, cos, sin):
    x32 = x.astype(jnp.float32)
    x1, x2 = x32[..., 0::2], x32[..., 1::2]
    c, s = cos[None, :, None, :], sin[None, :, None, :]
    out = jnp.stack([x1 * c - x2 * s, x1 * s + x2 * c], axis=-1).reshape(x.shape)
    return out.astype(x.dtype)

def multiscale_pool(u):
    B, S, _ = u.shape
    u32 = u.astype(jnp.float32)
    csum = jnp.concatenate([jnp.zeros((B, 1, POOL_DIM), jnp.float32), jnp.cumsum(u32, axis=1)], axis=1)
    t = jnp.arange(S)
    means = []
    for g, w in enumerate(POOL_WINDOWS):
        lo = jnp.clip(t - w // 2, 0, S)
        hi = jnp.clip(t + w - w // 2, 0, S)
        cg = csum[..., g * POOL_GROUP_DIM:(g + 1) * POOL_GROUP_DIM]
        total = jnp.take(cg, hi, axis=1) - jnp.take(cg, lo, axis=1)
        count = (hi - lo).astype(jnp.float32)
        means.append(total / count[None, :, None])
    return (jnp.concatenate(means, axis=-1) - u32).astype(u.dtype)

def grid_attention(q, k, v, cos, sin, q_gain, k_gain):
    q = apply_rope(rms_norm_2(q) * q_gain, cos, sin)
    k = apply_rope(rms_norm_2(k) * k_gain, cos, sin)
    B, S, H, Dh = q.shape
    G = H // ATT_KV_HEADS
    nb = S // Q_BLOCK
    qb = q.reshape(B, nb, Q_BLOCK, ATT_KV_HEADS, G, Dh).transpose(1, 0, 3, 4, 2, 5)
    kt = k.transpose(0, 2, 1, 3)
    vt = v.transpose(0, 2, 1, 3)
    scale = Dh ** -0.5

    def block(q_blk):
        s = jnp.einsum('bkgqd,bksd->bkgqs', q_blk, kt).astype(jnp.float32) * scale
        p = jax.nn.softmax(s, axis=-1).astype(vt.dtype)
        return jnp.einsum('bkgqs,bksd->bkgqd', p, vt)

    o = lax.map(block, qb)
    return o.transpose(1, 0, 4, 2, 3, 5).reshape(B, S, H * Dh)

def pool_attention_mixer(h, w_in, w_pool, b_pool, pool_scale, q_gain, k_gain, w_out, cos, sin):
    B, S, _ = h.shape
    z = h @ w_in
    u = z[..., :POOL_DIM]
    q = z[..., POOL_DIM:POOL_DIM + ATT_Q_DIM]
    k = z[..., POOL_DIM + ATT_Q_DIM:POOL_DIM + ATT_Q_DIM + ATT_KV_DIM]
    v = z[..., POOL_DIM + ATT_Q_DIM + ATT_KV_DIM:]
    pooled = multiscale_pool(u).reshape(B, S, N_POOL_GROUPS, POOL_GROUP_DIM)
    a = (jnp.einsum('bsgc,gcd->bsgd', pooled, w_pool) + b_pool).reshape(B, S, POOL_DIM) * pool_scale
    att = grid_attention(q.reshape(B, S, ATT_HEADS, ATT_HEAD_DIM),
                         k.reshape(B, S, ATT_KV_HEADS, ATT_HEAD_DIM),
                         v.reshape(B, S, ATT_KV_HEADS, ATT_HEAD_DIM),
                         cos, sin, q_gain, k_gain)
    return jnp.concatenate([a, att], axis=-1) @ w_out

def centred_depthwise_conv(u, w, b):
    y = lax.conv_general_dilated(u, w[:, None, :].astype(u.dtype), window_strides=(1,),
                                 padding=[(CONV_K // 2, CONV_K // 2)],
                                 dimension_numbers=('NWC', 'WIO', 'NWC'),
                                 feature_group_count=u.shape[-1])
    return y + b

def mlstm_chunkwise(q, k, v, log_i, log_f):
    q, k, v = (a.astype(jnp.float32) for a in (q, k, v))
    B, H, S, Dk = q.shape
    Dv = v.shape[-1]
    nc = S // CHUNK

    def to_chunks(a):
        return jnp.moveaxis(a.reshape(B, H, nc, CHUNK, *a.shape[3:]), 2, 0)

    qc, kc, vc, ic, fc = (to_chunks(a) for a in (q, k, v, log_i, log_f))
    lower = jnp.tril(jnp.ones((CHUNK, CHUNK), bool))

    def step(carry, inp):
        C, n, m = carry
        qj, kj, vj, ij, fj = inp
        b = jnp.cumsum(fj, axis=-1)
        a = b + m[..., None]
        D = jnp.where(lower, b[..., :, None] - b[..., None, :] + ij[..., None, :], -jnp.inf)
        m_t = jnp.maximum(a, jnp.max(D, axis=-1))
        w_inter = jnp.exp(a - m_t)
        s = jnp.einsum('bhtd,bhsd->bhts', qj, kj) * jnp.exp(D - m_t[..., None])
        num = jnp.einsum('bhts,bhsv->bhtv', s, vj) + w_inter[..., None] * jnp.einsum('bhvd,bhtd->bhtv', C, qj)
        den = jnp.sum(s, axis=-1) + w_inter * jnp.einsum('bhd,bhtd->bht', n, qj)
        h = num / jnp.maximum(jnp.abs(den), jnp.exp(-m_t))[..., None]
        bL = b[..., -1]
        g = bL[..., None] - b + ij
        m_new = jnp.maximum(bL + m, jnp.max(g, axis=-1))
        decay = jnp.exp(bL + m - m_new)
        wk = jnp.exp(g - m_new[..., None])
        C = decay[..., None, None] * C + jnp.einsum('bhsv,bhsd->bhvd', vj * wk[..., None], kj)
        n = decay[..., None] * n + jnp.einsum('bhs,bhsd->bhd', wk, kj)
        return (C, n, m_new), h

    init = (jnp.zeros((B, H, Dv, Dk), jnp.float32), jnp.zeros((B, H, Dk), jnp.float32),
            jnp.zeros((B, H), jnp.float32))
    _, hc = lax.scan(step, init, (qc, kc, vc, ic, fc))
    return jnp.moveaxis(hc, 0, 2).reshape(B, H, S, Dv)

def mlstm_mixer(h, w_in, conv_w, conv_b, gate_b, head_gain, w_out):
    B, S, _ = h.shape
    z = h @ w_in
    qk_raw = z[..., :2 * MLSTM_QK_WIDTH]
    v = z[..., 2 * MLSTM_QK_WIDTH:2 * MLSTM_QK_WIDTH + MLSTM_V_WIDTH]
    o = z[..., 2 * MLSTM_QK_WIDTH + MLSTM_V_WIDTH:2 * MLSTM_QK_WIDTH + 2 * MLSTM_V_WIDTH]
    gates = z[..., 2 * MLSTM_QK_WIDTH + 2 * MLSTM_V_WIDTH:]
    qk = jax.nn.silu(centred_depthwise_conv(qk_raw, conv_w, conv_b))
    q = qk[..., :MLSTM_QK_WIDTH].reshape(B, S, MLSTM_HEADS, MLSTM_QK_DIM).transpose(0, 2, 1, 3)
    k = (qk[..., MLSTM_QK_WIDTH:] * MLSTM_QK_DIM ** -0.5).reshape(B, S, MLSTM_HEADS, MLSTM_QK_DIM).transpose(0, 2, 1, 3)
    v = v.reshape(B, S, MLSTM_HEADS, MLSTM_V_DIM).transpose(0, 2, 1, 3)
    g = (gates.astype(jnp.float32) + gate_b.astype(jnp.float32)).reshape(B, S, 2, 2, MLSTM_HEADS)
    g = jnp.transpose(g, (2, 3, 0, 4, 1))
    h_fwd = mlstm_chunkwise(q, k, v, g[0, 0], jax.nn.log_sigmoid(g[0, 1]))
    flip = lambda a: jnp.flip(a, axis=2)
    h_bwd = flip(mlstm_chunkwise(flip(q), flip(k), flip(v), flip(g[1, 0]), flip(jax.nn.log_sigmoid(g[1, 1]))))
    hs = (h_fwd + h_bwd).transpose(0, 2, 1, 3).astype(h.dtype)
    hs = rms_norm_2(hs) * head_gain
    out = jax.nn.sigmoid(o).reshape(B, S, MLSTM_HEADS, MLSTM_V_DIM) * hs
    return out.reshape(B, S, MLSTM_V_WIDTH) @ w_out

def swiglu(h, w1, w3, w2):
    return (jax.nn.silu(h @ w1) * (h @ w3)) @ w2

def second_inputs(seed: int = 0) -> dict:
    key = jax.random.key(seed)
    ks = jax.random.split(key, 24)
    n_ev = (DEPTH_2 + 1) // 2
    n_od = DEPTH_2 // 2
    f32 = jnp.float32

    def nrm(k, shape, scale):
        return jax.random.normal(k, shape, f32) * scale

    i_bias = nrm(ks[14], (n_od, 2, MLSTM_HEADS), 0.1)
    f_bias = jnp.linspace(3.0, 6.0, MLSTM_HEADS, dtype=f32)[None, None, :] + nrm(ks[15], (n_od, 2, MLSTM_HEADS), 0.1)
    return {
        'x': nrm(ks[0], (BATCH, SEQ, D_MODEL), 1.0),
        'c': nrm(ks[1], (BATCH, D_MODEL), 1.0),
        'ada_w': nrm(ks[2], (DEPTH_2, D_MODEL, 6 * D_MODEL), D_MODEL ** -0.5),
        'ada_b': nrm(ks[3], (DEPTH_2, 6 * D_MODEL), 0.02),
        'ev_w_in': nrm(ks[4], (n_ev, D_MODEL, EVEN_IN_DIM), D_MODEL ** -0.5),
        'ev_w_pool': nrm(ks[5], (n_ev, N_POOL_GROUPS, POOL_GROUP_DIM, POOL_GROUP_DIM), POOL_GROUP_DIM ** -0.5),
        'ev_b_pool': nrm(ks[6], (n_ev, N_POOL_GROUPS, POOL_GROUP_DIM), 0.02),
        'ev_pool_scale': 1.0 + nrm(ks[7], (n_ev, POOL_DIM), 0.1),
        'ev_q_gain': 1.0 + nrm(ks[8], (n_ev, ATT_HEAD_DIM), 0.1),
        'ev_k_gain': 1.0 + nrm(ks[9], (n_ev, ATT_HEAD_DIM), 0.1),
        'ev_w_out': nrm(ks[10], (n_ev, EVEN_MIX_DIM, D_MODEL), EVEN_MIX_DIM ** -0.5),
        'od_w_in': nrm(ks[11], (n_od, D_MODEL, ODD_IN_DIM), D_MODEL ** -0.5),
        'od_conv_w': nrm(ks[12], (n_od, CONV_K, 2 * MLSTM_QK_WIDTH), CONV_K ** -0.5),
        'od_conv_b': nrm(ks[13], (n_od, 2 * MLSTM_QK_WIDTH), 0.02),
        'od_gate_b': jnp.stack([i_bias, f_bias], axis=2).reshape(n_od, N_GATES),
        'od_head_gain': 1.0 + nrm(ks[16], (n_od, MLSTM_HEADS, MLSTM_V_DIM), 0.1),
        'od_w_out': nrm(ks[17], (n_od, MLSTM_V_WIDTH, D_MODEL), MLSTM_V_WIDTH ** -0.5),
        'ffn_w1': nrm(ks[18], (DEPTH_2, D_MODEL, FFN_HIDDEN), D_MODEL ** -0.5),
        'ffn_w3': nrm(ks[19], (DEPTH_2, D_MODEL, FFN_HIDDEN), D_MODEL ** -0.5),
        'ffn_w2': nrm(ks[20], (DEPTH_2, FFN_HIDDEN, D_MODEL), FFN_HIDDEN ** -0.5),
    }

def second_block(x, c, ada_w, ada_b, ev_w_in, ev_w_pool, ev_b_pool, ev_pool_scale, ev_q_gain, ev_k_gain,
              ev_w_out, od_w_in, od_conv_w, od_conv_b, od_gate_b, od_head_gain, od_w_out,
              ffn_w1, ffn_w3, ffn_w2):
    cos, sin = grid_rope(x.shape[1])
    cond = jax.nn.silu(c)
    for layer in range(DEPTH_2):
        mod = cond @ ada_w[layer] + ada_b[layer]
        sh1, sc1, g1, sh2, sc2, g2 = jnp.split(mod, 6, axis=-1)
        h = modulate(rms_norm_2(x), sh1, sc1)
        j = layer // 2
        if layer % 2 == 0:
            y = pool_attention_mixer(h, ev_w_in[j], ev_w_pool[j], ev_b_pool[j], ev_pool_scale[j],
                                     ev_q_gain[j], ev_k_gain[j], ev_w_out[j], cos, sin)
        else:
            y = mlstm_mixer(h, od_w_in[j], od_conv_w[j], od_conv_b[j], od_gate_b[j],
                            od_head_gain[j], od_w_out[j])
        x = x + g1[:, None, :] * y
        h = modulate(rms_norm_2(x), sh2, sc2)
        x = x + g2[:, None, :] * swiglu(h, ffn_w1[layer], ffn_w3[layer], ffn_w2[layer])
    return x


def setup_inputs(seed=0):
    out = dict(first_inputs(seed))
    for name, value in second_inputs(seed + 1).items():
        if name != "x":
            out[name + "_2"] = value
    return out


def reference(
    x, norm_mix_g, w_in, b_gate, w_alpha_up, b_alpha, gla_norm_g, w_branch_sb, w_branch_gla,
    w_out, norm_ffn_g, w_ffn_in, conv_w, conv_b, w_ffn_out, norm_final_g, c_2, ada_w_2, ada_b_2,
    ev_w_in_2, ev_w_pool_2, ev_b_pool_2, ev_pool_scale_2, ev_q_gain_2, ev_k_gain_2, ev_w_out_2,
    od_w_in_2, od_conv_w_2, od_conv_b_2, od_gate_b_2, od_head_gain_2, od_w_out_2, ffn_w1_2,
    ffn_w3_2, ffn_w2_2,
):
    x = first_block(
        x, norm_mix_g, w_in, b_gate, w_alpha_up, b_alpha, gla_norm_g, w_branch_sb, w_branch_gla,
        w_out, norm_ffn_g, w_ffn_in, conv_w, conv_b, w_ffn_out, norm_final_g,
    )
    return second_block(
        x, c_2, ada_w_2, ada_b_2, ev_w_in_2, ev_w_pool_2, ev_b_pool_2, ev_pool_scale_2,
        ev_q_gain_2, ev_k_gain_2, ev_w_out_2, od_w_in_2, od_conv_w_2, od_conv_b_2, od_gate_b_2,
        od_head_gain_2, od_w_out_2, ffn_w1_2, ffn_w3_2, ffn_w2_2,
    )


_drawn_inputs = setup_inputs


def setup_inputs(seed=0):
    import zlib

    import numpy as np

    out = dict(_drawn_inputs(seed))
    spreads = {}
    factors = {'norm_mix_g': 2.862,
     'b_gate': 8.0,
     'b_alpha': 3.321,
     'gla_norm_g': 7.572,
     'norm_ffn_g': 3.556,
     'conv_b': 8.0,
     'ev_b_pool_2': 5.955,
     'ev_q_gain_2': 8.0,
     'ev_k_gain_2': 8.0,
     'od_conv_b_2': 24.249}
    for name, (base, spread) in spreads.items():
        noise = np.random.default_rng([zlib.crc32(name.encode()), seed]).standard_normal(out[name].shape)
        drawn = base * np.exp(spread * noise) if base else spread * noise
        out[name] = __import__('jax').numpy.asarray(drawn.astype(out[name].dtype))
    for name, factor in factors.items():
        out[name] = (out[name] * factor).astype(out[name].dtype)
    return out
```

```python
from contextlib import ExitStack
import math

import numpy as np
import concourse.bass as bass
from concourse import mybir

F = mybir.dt.float32
R = mybir.dt.float32r
ALU = mybir.AluOpType
ACT = mybir.ActivationFunctionType
AX_X = mybir.AxisListType.X

P = 128
T = 512
TB = T // P
D = 1024
KT = D // P
FF = 2816
HALF = FF // P // 2
EPS = 1e-6
NEG = -1e30
SP_CAP = 30.0

SB_H, SB_D = 8, 64
GLA_H, GLA_DV, GLA_C = 4, 128, 64
ATT_H = 8
ML_H = 8

PAR_COLS = {}
_n = 0
for _name, _w in (("norm_mix", KT), ("b_gate", 16), ("b_alpha", 2), ("gla_g", 4), ("norm_ffn", KT),
                  ("conv_w", 3 * 22), ("conv_b", 22), ("norm_final", KT), ("c", KT), ("ada_b", 96),
                  ("b_pool", 4), ("pool_scale", 4), ("q_gain", 1), ("k_gain", 1), ("od_conv_w", 40),
                  ("od_conv_b", 8), ("gate_b", 2), ("head_gain", 8), ("eps", 1)):
    PAR_COLS[_name] = (_n, _w)
    _n += _w
PAR_W = _n

CST_COLS = {}
_n = 0
for _name, _w in (("ident", P), ("ntri", P), ("ones", P), ("nones", P), ("neg_strict", P), ("keep_strict", P),
                  ("gla_mask", P), ("bd64", P), ("rot", P), ("neg_fwd", P), ("neg_bwd", P)):
    CST_COLS[_name] = (_n, _w)
    _n += _w
CST_W = _n
GLA_W = T + 256
ROPE_W = 2 * T
POOL_W = 5 * T
PAD = 8

WIDTH = {"F": 2048, "T": 2048, "KV": 2048, "S": 1024, "B": 1024, "D": HALF * P}
STAGES = [("sb_q", "F", 2), ("sb_k", "F", 2), ("sb_v", "T", 2),
          ("g_q", "F", 1), ("g_k", "F", 1),
          ("g_v", "T", 2), ("g_r", "F", 2), ("g_a", "S", 1), ("gates", "F", 8), ("branch", "B", 8),
          ("out", "F", 4), ("up0", "F", HALF), ("down0", "D", KT), ("up1", "F", HALF), ("down1", "D", KT),
          ("pool_u", "F", 2), ("att_q", "F", 2), ("att_kv", "KV", 1), ("att_out", "F", 4),
          ("e_up0", "F", HALF), ("e_down0", "D", KT), ("e_up1", "F", HALF), ("e_down1", "D", KT),
          ("ml_qk", "F", 4), ("ml_v", "T", 4), ("ml_g", "S", 1), ("ml_o", "F", 4), ("ml_out", "F", 4),
          ("o_up0", "F", HALF), ("o_down0", "D", KT), ("o_up1", "F", HALF), ("o_down1", "D", KT)]
C0, KIND, COUNT = {}, {}, {}
_c = 0
for _name, _k, _cnt in STAGES:
    C0[_name], KIND[_name], COUNT[_name] = _c, _k, _cnt
    _c += _cnt
N_CHUNKS = _c
ROW0, ROWS = {}, {}
for _name, _k, _cnt in STAGES:
    ROW0[_name] = ROWS.get(WIDTH[_k], 0)
    ROWS[WIDTH[_k]] = ROW0[_name] + _cnt
ADA_N = 24


def end_of(stage):
    return C0[stage] + COUNT[stage]


def build(nc, xT, w2048, w1024, w1408, ada, par_d, cst_d, gla_d, rope_d, pool_d, outT):
    with ExitStack() as ctx:
        def sb(name, shape, dt=F):
            return ctx.enter_context(nc.sbuf_tensor(name, shape, dt))

        def sem(name):
            return ctx.enter_context(nc.semaphore(name))

        h = sb("h", [P, KT, T])
        xh, xl = sb("xh", [P, KT, T], R), sb("xl", [P, KT, T], R)
        raw = sb("raw", [P, 2, 2048])
        wh, wl = sb("wh", [P, 2, 2048], R), sb("wl", [P, 2, 2048], R)
        zh, zl = sb("zh", [P, HALF, T], R), sb("zl", [P, HALF, T], R)
        par, cst = sb("par", [P, PAR_W]), sb("cst", [P, CST_W])
        mod = sb("mod", [P, 2, 48])
        cond = sb("cond", [P, KT])
        small = sb("small", [P, 256])
        arena = sb("arena", [P, 28, T])
        pairs = ctx.enter_context(nc.psum_tensor("pairs", [P, 4, T], F))
        aux = ctx.enter_context(nc.psum_tensor("aux", [P, 4, T], F))

        def pc(name, i=0, n=1):
            return par[:, PAR_COLS[name][0] + i:PAR_COLS[name][0] + i + n]

        def pc_at(name, i):
            return par[:, bass.ds(i + PAR_COLS[name][0], 1)]

        def cm(name):
            return cst[:, CST_COLS[name][0]:CST_COLS[name][0] + CST_COLS[name][1]]

        raw_full = [sem("raw_full0"), sem("raw_full1")]
        hi_done, lo_done = sem("hi_done"), sem("lo_done")
        mm_done = sem("mm_done")
        drained = sem("drained")
        consts = sem("consts")
        x_in = sem("x_in")
        stored = sem("stored")

        def chunk_loop(eng, stage, body, lo=0, hi=None):
            c0 = C0[stage]
            c, end = c0 + lo, c0 + (COUNT[stage] if hi is None else hi)
            while c < end and c < 2:
                body(c, c % 2, c - c0)
                c += 1
            pairs_n = (end - c) // 2
            if pairs_n > 1:
                with eng.Fori(0, pairs_n) as i:
                    body(i * 2 + c, c % 2, i * 2 + (c - c0))
                    body(i * 2 + (c + 1), (c + 1) % 2, i * 2 + (c + 1 - c0))
            elif pairs_n == 1:
                body(c, c % 2, c - c0)
                body(c + 1, (c + 1) % 2, c + 1 - c0)
            c += 2 * pairs_n
            if c < end:
                body(c, c % 2, c - c0)

        def is_static(c):
            return isinstance(c, int)

        S = {}

        def s(name):
            if name not in S:
                S[name] = sem(name)
            return S[name]

        NORM_OF = {"n_mix": 0, "n_ffn": 1, "n_final": 2, "n_e1": 3, "n_e2": 4, "n_o1": 5, "n_o2": 6}
        NORM_AFTER = {"n_mix": None, "n_ffn": "out", "n_final": "down1", "n_e1": None, "n_e2": "att_out",
                      "n_o1": "e_down1", "n_o2": "ml_out"}
        sq_done, sq_used = s("sq_done"), s("sq_used")
        rstd_done = s("rstd_done")
        xn_done, xh_done, x_ready = s("xn_done"), s("xh_done"), s("x_ready")
        h_final = s("h_final")
        SQ = arena[:, 0:2, :]
        RSTD = arena[:, 2, :]
        LNV = arena[:, 3, :]
        XN = arena[:, 4:6, :]

        def norm_cols(name):
            if name in ("n_mix", "n_ffn", "n_final"):
                key = {"n_mix": "norm_mix", "n_ffn": "norm_ffn", "n_final": "norm_final"}[name]
                return (lambda k: pc(key, k)), None
            layer, second = (0, 1) if name[2] == "e" else (1, 1)
            base = 0 if name[3] == "1" else 24
            return ((lambda k: mod[:, layer, base + 8 + k:base + 9 + k]),
                    (lambda k: mod[:, layer, base + k:base + k + 1]))

        def norm_act(a, name):
            n = NORM_OF[name]
            if name == "n_mix":
                a.wait_ge(consts, 32)
                a.wait_ge(x_in, 16)
            elif name == "n_e1":
                a.wait_ge(h_final, KT)
            else:
                a.wait_ge(drained, end_of(NORM_AFTER[name]))
            for k in range(KT):
                if KT * n + k >= 2:
                    a.wait_ge(sq_used, KT * n + k - 1)
                a.activation(SQ[:, k % 2, :], h[:, k, :], ACT.Square).then_inc(sq_done, 1)
            a.preload_act_table_set("natural_log_exp_and_others")
            a.wait_ge(sq_used, KT * (n + 1))
            a.activation(LNV, aux[:, 0, :], ACT.Ln, scale=1.0 / D, bias=pc("eps")).then_inc(s("norm_ln"), 1)
            a.wait_ge(s("norm_ln"), n + 1)
            a.activation(RSTD, LNV, ACT.Exp, scale=-0.5).then_inc(rstd_done, 1)
            if name == "n_final":
                return
            _, shift = norm_cols(name)
            m = n if n < 2 else n - 1
            for k in range(KT):
                a.wait_ge(xn_done, KT * m + k + 1)
                if shift is None:
                    a.activation(xh[:, k, :], XN[:, k % 2, :], ACT.Copy).then_inc(xh_done, 1)
                else:
                    a.activation(xh[:, k, :], XN[:, k % 2, :], ACT.Identity, bias=shift(k)).then_inc(xh_done, 1)

        def norm_pe(p, name):
            n = NORM_OF[name]
            if n == 0:
                p.wait_ge(consts, 32)
            if n:
                p.wait_ge(rstd_done, n)
            for k in range(KT):
                p.wait_ge(sq_done, KT * n + k + 1)
                p.matmul(aux[:, 0, :], cm("ones"), SQ[:, k % 2, :], start=(k == 0), stop=(k == KT - 1)
                         ).then_inc(sq_used, 1)

        def norm_dve(v, name):
            n = NORM_OF[name]
            scale, shift = norm_cols(name)
            v.wait_ge(rstd_done, n + 1)
            if name == "n_final":
                for k in range(KT):
                    v.scalar_tensor_tensor(h[:, k, :], h[:, k, :], scale(k), RSTD, ALU.mult, ALU.mult
                                           ).then_inc(h_final, 1)
                return
            m = n if n < 2 else n - 1
            for k in range(KT + 1):
                if k < KT:
                    if k >= 2:
                        v.wait_ge(x_ready, KT * m + k - 1)
                    v.scalar_tensor_tensor(XN[:, k % 2, :], h[:, k, :], scale(k), RSTD, ALU.mult, ALU.mult
                                           ).then_inc(xn_done, 1)
                if k:
                    v.wait_ge(xh_done, KT * m + k)
                    src, dst = XN[:, (k - 1) % 2, :], xl[:, k - 1, :]
                    hi = xh[:, k - 1, :].bitcast(F)
                    if shift is None:
                        v.tensor_tensor(dst, src, hi, ALU.subtract).then_inc(x_ready, 1)
                    else:
                        v.scalar_tensor_tensor(dst, src, shift(k - 1), hi, ALU.add, ALU.subtract
                                               ).then_inc(x_ready, 1)

        def hi_part(a, c, slot):
            a.wait_ge(raw_full[slot], c * 8 + (16 if slot == 0 else 8))
            if not (is_static(c) and c < 2):
                a.wait_ge(mm_done, c - 1)
            a.activation(wh[:, slot, :], raw[:, slot, :], ACT.Copy).then_inc(hi_done, 1)

        def linear_pe(p, stage, ready=None):
            kind = KIND[stage]
            if ready:
                p.wait_ge(*ready)
            passes = ((wh, 0), (wl, 0), (wh, 1))

            def body(c, slot, l):
                p.wait_ge(lo_done, c + 1)
                if not (is_static(c) and c < 2):
                    p.wait_ge(drained, c - 1)
                src = (zh, zl) if stage in ("att_out", "ml_out") else (xh, xl)
                if kind in ("F", "KV"):
                    for m in range(2 if kind == "F" else 1):
                        for k in range(KT):
                            for w, part in passes:
                                at = k * 256 + m * P
                                mm = p.matmul(pairs[:, 2 * slot + m, :], w[:, slot, at:at + P], src[part][:, k, :],
                                              start=(k == 0 and w is wh and part == 0),
                                              stop=(k == KT - 1 and part == 1))
                if kind in ("T", "KV"):
                    n = 256 if kind == "T" else P
                    for tb in range(TB):
                        if kind == "T":
                            dst = pairs[:, 2 * slot + tb // 2, (tb % 2) * 256:(tb % 2) * 256 + 256]
                        else:
                            dst = pairs[:, 2 * slot + 1, tb * P:(tb + 1) * P]
                        for k in range(KT):
                            for w, part in passes:
                                at = k * 256 + (0 if kind == "T" else P)
                                mm = p.matmul(dst, src[part][:, k, tb * P:(tb + 1) * P], w[:, slot, at:at + n],
                                              start=(k == 0 and w is wh and part == 0),
                                              stop=(k == KT - 1 and part == 1))
                if kind in ("S", "B", "D"):
                    src = (xh, xl) if kind == "S" else (zh, zl)
                    tiles = {"S": [range(KT)], "B": [range(4), range(4, 8)], "D": [range(HALF)]}[kind]
                    for m, ks in enumerate(tiles):
                        for k in ks:
                            for w, part in passes:
                                mm = p.matmul(pairs[:, 2 * slot + m, :], w[:, slot, k * P:(k + 1) * P],
                                              src[part][:, k, :],
                                              start=(k == ks[0] and w is wh and part == 0),
                                              stop=(k == ks[-1] and part == 1))
                mm.then_inc(mm_done, 1)
                if stage in ADA_OF:
                    ada_pe(p, l + ADA_OF[stage], ada_slot(stage, slot), 0 if ADA_OF[stage] < ADA_N else 1)
            chunk_loop(p, stage, body)

        def hi_only(a, stage):
            last = 1 if end_of(stage) == N_CHUNKS else 0
            chunk_loop(a, stage, lambda c, slot, l: hi_part(a, c + 1, 1 - slot), hi=COUNT[stage] - last)

        def drain_copy(v, stage, dst, scale=1.0):
            def body(c, slot, l):
                v.wait_ge(mm_done, c + 1)
                src = pairs[:, 2 * slot:2 * slot + 2, :]
                if KIND[stage] == "T":
                    src = src.rearrange("p b (t n) -> p (b t) n", n=256)
                v.tensor_scalar(dst(l), src, scale, None, ALU.mult).then_inc(drained, 1)
            chunk_loop(v, stage, body)

        def drain_residual(v, stage, gate=None):
            def body(c, slot, l):
                v.wait_ge(mm_done, c + 1)
                if KIND[stage] == "D":
                    tile = h[:, bass.ds(l, 1), :]
                    if gate is None:
                        v.tensor_tensor(tile, pairs[:, 2 * slot:2 * slot + 1, :], tile, ALU.add).then_inc(drained, 1)
                    else:
                        v.scalar_tensor_tensor(tile, pairs[:, 2 * slot:2 * slot + 1, :], gate(l), tile,
                                               ALU.mult, ALU.add).then_inc(drained, 1)
                elif gate is None:
                    tile = h[:, bass.ds(l * 2, 2), :]
                    v.tensor_tensor(tile, pairs[:, 2 * slot:2 * slot + 2, :], tile, ALU.add).then_inc(drained, 1)
                else:
                    for m in range(2):
                        tile = h[:, bass.ds(l * 2 + m, 1), :]
                        ins = v.scalar_tensor_tensor(tile, pairs[:, 2 * slot + m:2 * slot + m + 1, :],
                                                     gate(l * 2 + m), tile, ALU.mult, ALU.add)
                    ins.then_inc(drained, 1)
            chunk_loop(v, stage, body)

        UP_N = {"up0": 0, "up1": 1, "e_up0": 2, "e_up1": 3, "o_up0": 4, "o_up1": 5}
        a_copied, conv_done, act_done = s("a_copied"), s("conv_done"), s("act_done")
        hid_done, hid_hi, conv_step = s("hid_done"), s("hid_hi"), s("conv_step")
        APAD = arena[:, 0:4, :].rearrange("p a b -> p (a b)")
        apad = [APAD[:, i * 1024:i * 1024 + T + 2] for i in range(2)]
        CONV = arena[:, 4:6, :]
        ACTV = arena[:, 6:8, :]
        HID = arena[:, 8:10, :]

        def up_act(a, stage):
            first = stage in ("up0", "up1")
            n0 = UP_N[stage] * HALF

            def body(c, slot, l):
                hi_part(a, c + 1, 1 - slot)
                a.wait_ge(mm_done, c + 1)
                f = l + n0
                if first:
                    a.activation(apad[slot][:, 2:T + 2], pairs[:, 2 * slot, :], ACT.Copy).then_inc(a_copied, 1)
                    a.wait_ge(conv_done, f + 1)
                    a.activation(ACTV[:, slot, :], CONV[:, slot, :], ACT.Gelu_apprx_tanh).then_inc(act_done, 1)
                else:
                    a.activation(ACTV[:, slot, :], pairs[:, 2 * slot, :], ACT.Silu).then_inc(act_done, 1)
                a.wait_ge(hid_done, f + 1)
                a.wait_ge(consts, 32)
                a.activation(zh[:, bass.ds(l, 1), :], HID[:, slot:slot + 1, :], ACT.Copy).then_inc(hid_hi, 1)
            chunk_loop(a, stage, body)

        def up_dve(v, stage):
            first = stage in ("up0", "up1")
            n0 = UP_N[stage] * HALF
            half = HALF if stage in ("up1",) else 0

            def body(c, slot, l):
                f = l + n0
                if stage in ADA_OF:
                    ada_dve(v, l + ADA_OF[stage], ada_slot(stage, slot))
                if first:
                    v.wait_ge(a_copied, f + 1)
                    w = lambda tap: pc_at("conv_w", l + (tap * 22 + half))
                    v.tensor_scalar(CONV[:, slot, :], apad[slot][:, 0:T], w(0), pc_at("conv_b", l + half),
                                    ALU.mult, ALU.add).then_inc(conv_step, 1)
                    v.wait_ge(conv_step, f * 2 + 1)
                    v.scalar_tensor_tensor(CONV[:, slot, :], apad[slot][:, 1:T + 1], w(1), CONV[:, slot, :],
                                           ALU.mult, ALU.add).then_inc(conv_step, 1)
                    v.wait_ge(conv_step, f * 2 + 2)
                    v.scalar_tensor_tensor(CONV[:, slot, :], apad[slot][:, 2:T + 2], w(2), CONV[:, slot, :],
                                           ALU.mult, ALU.add).then_inc(conv_done, 1)
                v.wait_ge(act_done, f + 1)
                v.tensor_tensor(HID[:, slot, :], ACTV[:, slot, :], pairs[:, 2 * slot + 1, :], ALU.mult
                                ).then_inc(hid_done, 1)
                v.wait_ge(hid_hi, f + 1)
                v.tensor_tensor(zl[:, bass.ds(l, 1), :], HID[:, slot:slot + 1, :],
                                zh[:, bass.ds(l, 1), :].bitcast(F), ALU.subtract).then_inc(drained, 1)
            chunk_loop(v, stage, body)

        ada_full = [sem("ada_full0"), sem("ada_full1")]
        ada_step, ada_acc_done, ada_sum = sem("ada_step"), sem("ada_acc_done"), sem("ada_sum")
        ada_raw = arena[:, 10:18, :].rearrange("p (s x) b -> p s (x b)", s=2)
        ada_acc = sb("ada_acc", [P, 2, 256])
        ADA_OF = {"up0": 2, "up1": 2 + HALF, "e_up0": ADA_N + 2, "e_up1": ADA_N + 2 + HALF}

        def ada_load(sp, A, slot):
            if not (is_static(A) and A < 2):
                sp.wait_ge(ada_acc_done, A - 1)
            sp.dma_start(ada_raw[:, slot, :], ada[bass.ds(A, 1), :, :].rearrange("a p n -> p (a n)")
                         ).then_inc(ada_full[slot], 16)

        def ada_dve(v, A, slot):
            v.wait_ge(ada_full[slot], A * 8 + (16 if slot == 0 else 8))
            if not (is_static(A) and A < 2):
                v.wait_ge(ada_sum, A - 1)
            acc = ada_acc[:, slot, :]
            v.tensor_scalar(acc, ada_raw[:, slot, 0:256], cond[:, 0:1], None, ALU.mult).then_inc(ada_step, 1)
            for k in range(1, KT):
                v.wait_ge(ada_step, A * (KT - 1) + k)
                v.scalar_tensor_tensor(acc, ada_raw[:, slot, k * 256:(k + 1) * 256], cond[:, k:k + 1], acc,
                                       ALU.mult, ALU.add).then_inc(ada_step if k < KT - 1 else ada_acc_done, 1)

        def ada_pe(p, A, slot, layer):
            p.wait_ge(ada_acc_done, A + 1)
            for m in range(2):
                mm = p.matmul(aux[:, 1, bass.ds((A - layer * ADA_N) * 2 + m, 1)], ada_acc[:, slot, m * P:(m + 1) * P],
                              cm("ones")[:, 0:1], start=True, stop=True)
            mm.then_inc(ada_sum, 1)

        def ada_slot(stage, slot):
            return (slot + C0[stage] + ADA_OF[stage]) % 2

        mod_done = sem("mod_done")

        def mod_dve(v, layer):
            v.wait_ge(ada_sum, ADA_N * (layer + 1))
            v.tensor_tensor(mod[:, layer, :], aux[:, 1, 0:48], pc("ada_b", 48 * layer, 48), ALU.add
                            ).then_inc(mod_done, 1)
            v.wait_ge(mod_done, 2 * layer + 1)
            two = mod[:, layer, :].rearrange("p (a b) -> p a b", a=2)[:, :, 8:16]
            v.tensor_scalar(two, two, 1.0, None, ALU.add).then_inc(mod_done, 1)

        SBQ, SBK = arena[:, 0:4, :], arena[:, 4:8, :]
        SBV = arena[:, 8:12, :]
        SB_EL = arena[:, 12:14, :]
        SB_W = arena[:, 14:16, :]
        SB_SPA = arena[:, 16:19, :].rearrange("p a b -> p (a b)")
        sp_at = [0, 512, 896, 1152]
        SB_SP = [SB_SPA[:, sp_at[i]:sp_at[i] + T - P * i] for i in range(TB)]
        b_qk, b_cap, b_exp, b_ln = sem("b_qk"), sem("b_cap"), sem("b_exp"), sem("b_ln")
        b_max, b_sp, b_tri, b_w, b_pv = sem("b_max"), sem("b_sp"), sem("b_tri"), sem("b_w"), sem("b_pv")
        z_hi, z_lo = sem("z_hi"), sem("z_lo")

        SB_N = SB_H * TB

        def sb_pe(p):
            p.wait_ge(drained, end_of("sb_v"))

            def qk(n):
                hd, i = n // TB, TB - 1 - n % TB
                r = (hd % 2) * SB_D
                if n >= 3:
                    p.wait_ge(b_w, n - 2)
                p.matmul(aux[:, n % 3, 0:T - P * i], SBK[r:r + SB_D, hd // 2, i * P:(i + 1) * P],
                         SBQ[r:r + SB_D, hd // 2, i * P:T], start=True, stop=True).then_inc(b_qk, 1)

            def tri(n):
                hd, i = n // TB, TB - 1 - n % TB
                w = T - P * i
                p.wait_ge(b_sp, n + 1)
                p.matmul(aux[:, n % 3, 0:w], cm("ntri"), SB_SP[i], start=False, stop=False,
                         skip_group_check=True)
                for j in range(i + 1, TB):
                    p.matmul(aux[:, n % 3, (j - i) * P:w], cm("nones"), SB_SP[j], start=False, stop=False,
                             skip_group_check=True)
                p.matmul(aux[:, n % 3, 0:P], cm("ident"), cm("neg_strict"), start=False, stop=True,
                         skip_group_check=True).then_inc(b_tri, 1)

            def pv(n):
                hd, i = n // TB, TB - 1 - n % TB
                r = (hd % 2) * SB_D
                p.wait_ge(b_w, n + 1)
                if n % (2 * TB) == 0 and n:
                    p.wait_ge(z_lo, n // (2 * TB))
                p.matmul(aux[r:r + SB_D, 3, i * P:T], SBV[:, i, hd * SB_D:(hd + 1) * SB_D], SB_W[:, n % 2, 0:T - P * i],
                         start=(i == TB - 1), stop=(i == 0), skip_group_check=True).then_inc(b_pv, 1)

            qk(0)
            qk(1)
            for n in range(SB_N):
                tri(n)
                if n:
                    pv(n - 1)
                if n + 2 < SB_N:
                    qk(n + 2)
            pv(SB_N - 1)

        def sb_act(a):
            a.preload_act_table_set("natural_log_exp_and_others")

            def weights(n):
                w = T - P * (TB - 1 - n % TB)
                a.wait_ge(b_tri, n + 1)
                if n >= 2:
                    a.wait_ge(b_pv, n - 1)
                a.activation(SB_W[:, n % 2, 0:w], aux[:, n % 3, 0:w], ACT.Exp).then_inc(b_w, 1)

            def out_hi(pr):
                a.wait_ge(b_pv, 2 * TB * (pr + 1))
                a.activation(zh[:, pr, :], aux[:, 3, :], ACT.Copy).then_inc(z_hi, 1)

            for n in range(SB_N):
                w = T - P * (TB - 1 - n % TB)
                el = SB_EL[:, n % 2, 0:w]
                a.wait_ge(b_cap, n + 1)
                a.activation(el, el, ACT.Exp).then_inc(b_exp, 1)
                a.wait_ge(b_exp, n + 1)
                a.activation(el, el, ACT.Ln, bias=1.0).then_inc(b_ln, 1)
                if n:
                    weights(n - 1)
                if n % (2 * TB) == 1 and n > 1:
                    out_hi(n // (2 * TB) - 1)
            weights(SB_N - 1)
            out_hi(SB_H // 2 - 1)

        def sb_dve(v):
            def out_lo(pr):
                v.wait_ge(z_hi, pr + 1)
                v.tensor_tensor(zl[:, pr, :], aux[:, 3, :], zh[:, pr, :].bitcast(F), ALU.subtract).then_inc(z_lo, 1)

            for n in range(SB_N):
                i = TB - 1 - n % TB
                w = T - P * i
                el = SB_EL[:, n % 2, 0:w]
                v.wait_ge(b_qk, n + 1)
                v.tensor_scalar(el, aux[:, n % 3, 0:w], SP_CAP, None, ALU.min).then_inc(b_cap, 1)
                v.wait_ge(b_ln, n + 1)
                if n % TB == 0 and n:
                    v.wait_ge(b_tri, n)
                elif n:
                    if n >= TB:
                        v.wait_ge(b_tri, n - n % TB)
                v.tensor_tensor(SB_SP[i], aux[:, n % 3, 0:w], el, ALU.max).then_inc(b_max, 1)
                v.wait_ge(b_max, n + 1)
                v.tensor_tensor(SB_SP[i][:, 0:P], SB_SP[i][:, 0:P], cm("keep_strict"), ALU.mult).then_inc(b_sp, 1)
                if n % (2 * TB) == 1 and n > 1:
                    out_lo(n // (2 * TB) - 1)
            out_lo(SB_H // 2 - 1)

        GQ, GK = arena[:, 0:2, :], arena[:, 2:4, :]
        GV = arena[:, 4:8, :]
        GR = arena[:, 8:12, :]
        G_NX, G_EL, G_CUM = arena[:, 12:14, :], arena[:, 14:16, :], arena[:, 16:18, :]
        G_EQ, G_EK, G_EE = arena[:, 18:20, :], arena[:, 20:22, :], arena[:, 22:24, :]
        G_A = arena[:, 24, :]
        G_CST = arena[:, 25:27, :].rearrange("p a b -> p (a b)")
        G_RESET, G_WA = G_CST[:, 0:T], G_CST[:, T:T + 256]
        G_KT = G_NX
        G_S = arena[:, 24:28, :].rearrange("p (j x) (n v) -> p j (x n) v", j=2, v=P)
        G_AT = [arena[:, 14, :], arena[:, 15, :], arena[:, 20, :], arena[:, 21, :]]
        G_SQ, G_RS, G_T = G_CUM, G_NX, G_EE
        gla_in = sem("gla_in")
        g_pre, g_nx, g_cap, g_e, g_l = sem("g_pre"), sem("g_nx"), sem("g_cap"), sem("g_e"), sem("g_l")
        g_sp, g_cum, g_eqk, g_diff, g_ee = sem("g_sp"), sem("g_cum"), sem("g_eqk"), sem("g_diff"), sem("g_ee")
        g_qd, g_ki, g_ke, g_tr, g_kt = sem("g_qd"), sem("g_ki"), sem("g_ke"), sem("g_tr"), sem("g_kt")
        g_att, g_at, g_ds, g_st, g_o = sem("g_att"), sem("g_at"), sem("g_ds"), sem("g_st"), sem("g_o")
        g_sq, g_ms, g_ln, g_rs, g_t1 = sem("g_sq"), sem("g_ms"), sem("g_ln"), sem("g_rs"), sem("g_t1")
        g_t2, g_silu = sem("g_t2"), sem("g_silu")
        GN = T // GLA_C
        STEPS = [(j, c) for j in range(2) for c in range(GN - 1)]
        g_in = sem("g_in")

        def gla_pe(p):
            p.wait_ge(drained, end_of("g_a"))
            p.wait_ge(gla_in, 16)
            for j in range(2):
                p.matmul(aux[:, j, :], G_WA[0:16, j * P:(j + 1) * P], G_A[0:16, :], start=True, stop=True
                         ).then_inc(g_pre, 1)
            for j in range(2):
                p.wait_ge(g_ke, 1)
                for tb in range(TB):
                    mm = p.transpose(aux[:, 2 + j, tb * P:(tb + 1) * P], G_EE[:, j, tb * P:(tb + 1) * P], cm("ident"))
                mm.then_inc(g_tr, 1)
            p.wait_ge(g_ki, 1)
            for hd in range(GLA_H):
                r, j = (hd % 2) * 64, hd // 2
                if hd >= 2:
                    p.wait_ge(g_at, hd - 1)
                for tb in range(TB):
                    c = slice(tb * P, (tb + 1) * P)
                    mm = p.matmul(aux[:, hd % 2, c], GK[r:r + 64, j, c], GQ[r:r + 64, j, c], start=True, stop=True)
                mm.then_inc(g_att, 1)
            p.wait_ge(g_kt, 2)
            for n, (j, c) in enumerate(STEPS):
                r, k = (c % 2) * 64, c // 2
                if n >= 2:
                    p.wait_ge(g_st, n - 1 if c else n)
                p.matmul(aux[:, 2 + c % 2, 0:256], G_KT[r:r + 64, j, k * P:(k + 1) * P],
                         GV[r:r + 64, k, j * 256:(j + 1) * 256], start=True, stop=True).then_inc(g_ds, 1)
            p.wait_ge(g_st, 2 * (GN - 1))
            for hd in range(GLA_H + 1):
                if hd < GLA_H:
                    r, j = (hd % 2) * 64, hd // 2
                    p.wait_ge(g_at, GLA_H)
                    if hd >= 2:
                        p.wait_ge(g_t1, hd - 1)
                    for tb in range(TB):
                        c = slice(tb * P, (tb + 1) * P)
                        mm = p.matmul(aux[:, hd % 2, c], GV[:, tb, hd * P:(hd + 1) * P], G_AT[hd][:, c],
                                      start=(tb == 0), stop=True, skip_group_check=True)
                    mm.then_inc(g_in, 1)
                    p.wait_ge(g_in, hd + 1)
                    for n in range(1, GN):
                        mm = p.matmul(aux[:, hd % 2, n * 64:(n + 1) * 64], G_S[r:r + 64, j, n, :],
                                      GQ[r:r + 64, j, n * 64:(n + 1) * 64], start=False, stop=True,
                                      skip_group_check=True)
                    mm.then_inc(g_o, 1)
                if hd:
                    q = hd - 1
                    p.wait_ge(g_sq, q + 1)
                    if q >= 2:
                        p.wait_ge(g_ln, q - 1)
                    p.matmul(aux[:, 2 + q % 2, :], cm("ones"), G_SQ[:, q % 2, :], start=True, stop=True
                             ).then_inc(g_ms, 1)

        def gla_act(a):
            a.wait_ge(drained, end_of("g_r"))
            a.activation(GR, GR, ACT.Silu).then_inc(g_silu, 1)
            a.preload_act_table_set("natural_log_exp_and_others")
            a.wait_ge(g_cap, 1)
            a.activation(G_EL, G_EL, ACT.Exp).then_inc(g_e, 1)
            a.wait_ge(g_e, 1)
            a.activation(G_EL, G_EL, ACT.Ln, bias=1.0).then_inc(g_l, 1)
            a.wait_ge(g_cum, 2)
            a.activation(G_EQ, G_CUM, ACT.Exp, scale=-1.0 / 16).then_inc(g_eqk, 1)
            a.activation(G_EK, G_CUM, ACT.Exp, scale=1.0 / 16).then_inc(g_eqk, 1)
            a.wait_ge(g_diff, 1)
            a.activation(G_EE, G_EE, ACT.Exp, scale=-1.0 / 16).then_inc(g_ee, 1)
            for hd in range(GLA_H + 1):
                if hd < GLA_H:
                    a.wait_ge(g_o, hd + 1)
                    if hd >= 2:
                        a.wait_ge(g_ms, hd - 1)
                    a.activation(G_SQ[:, hd % 2, :], aux[:, hd % 2, :], ACT.Square).then_inc(g_sq, 1)
                if hd:
                    q = hd - 1
                    a.wait_ge(g_ms, q + 1)
                    if q >= 2:
                        a.wait_ge(g_t1, q - 1)
                    rs = G_RS[:, q % 2, :]
                    a.activation(rs, aux[:, 2 + q % 2, :], ACT.Ln, scale=1.0 / GLA_DV, bias=pc("eps")).then_inc(g_ln, 1)
                    a.wait_ge(g_ln, q + 1)
                    a.activation(rs, rs, ACT.Exp, scale=-0.5).then_inc(g_rs, 1)
                    a.wait_ge(g_t2, q + 1)
                    a.activation(zh[:, 4 + q, :], G_T[:, q % 2, :], ACT.Copy).then_inc(z_hi, 1)

        def gla_dve(v):
            v.wait_ge(g_pre, 2)
            v.wait_ge(gla_in, 16)
            for j in range(2):
                v.tensor_scalar(G_NX[:, j, :], aux[:, j, :], -1.0, pc("b_alpha", j), ALU.mult, ALU.subtract
                                ).then_inc(g_nx, 1)
            v.wait_ge(g_nx, 2)
            v.tensor_scalar(G_EL, G_NX, SP_CAP, None, ALU.min).then_inc(g_cap, 1)
            v.wait_ge(g_l, 1)
            v.tensor_tensor(G_NX, G_NX, G_EL, ALU.max).then_inc(g_sp, 1)
            v.wait_ge(g_sp, 1)
            for j in range(2):
                v.tensor_tensor_scan(G_CUM[:, j, :], G_RESET, G_NX[:, j, :], 0.0, ALU.mult, ALU.add
                                     ).then_inc(g_cum, 1)
            v.wait_ge(g_cum, 2)
            cum = G_CUM.rearrange("p j (n c) -> p (j n) c", c=GLA_C)
            v.tensor_tensor(G_EE.rearrange("p j (n c) -> p (j n) c", c=GLA_C),
                            cum[:, :, GLA_C - 1:GLA_C].to_broadcast([P, 2 * GN, GLA_C]), cum, ALU.subtract
                            ).then_inc(g_diff, 1)
            v.wait_ge(g_ee, 1)
            v.tensor_tensor(G_EE, GK, G_EE, ALU.mult).then_inc(g_ke, 1)
            v.wait_ge(g_eqk, 2)
            v.tensor_tensor(GQ, GQ, G_EQ, ALU.mult)
            v.wait_ge(g_ke, 1)
            v.tensor_tensor(GK, GK, G_EK, ALU.mult).then_inc(g_ki, 1)
            v.wait_ge(g_tr, 2)
            v.tensor_copy(G_KT, aux[:, 2:4, :]).then_inc(g_kt, 2)
            v.wait_ge(g_ki, 1)
            for hd in range(GLA_H):
                v.wait_ge(g_att, hd + 1)
                v.tensor_tensor(G_AT[hd].rearrange("p (b c) -> p b c", c=P),
                                aux[:, hd % 2, :].rearrange("p (b c) -> p b c", c=P),
                                cm("gla_mask").rearrange("p (a c) -> p a c", a=1).to_broadcast([P, TB, P]), ALU.mult
                                ).then_inc(g_at, 1)
            for n, (j, c) in enumerate(STEPS):
                v.wait_ge(g_ds, n + 1)
                if c:
                    v.wait_ge(g_st, n)
                for r in (0, 64):
                    inc = aux[r:r + 64, 2 + c % 2, 2 * r:2 * r + P]
                    new = G_S[r:r + 64, j, c + 1, :]
                    if c == 0:
                        ins = v.tensor_copy(new, inc)
                    else:
                        end = c * GLA_C + GLA_C - 1
                        ins = v.scalar_tensor_tensor(new, G_S[r:r + 64, j, c, :], G_EQ[r:r + 64, j, end:end + 1],
                                                     inc, ALU.mult, ALU.add)
                ins.then_inc(g_st, 1)
            v.wait_ge(g_silu, 1)
            for hd in range(GLA_H):
                v.wait_ge(g_rs, hd + 1)
                if hd >= 2:
                    v.wait_ge(z_lo, 4 + hd - 1)
                t = G_T[:, hd % 2, :]
                v.scalar_tensor_tensor(t, aux[:, hd % 2, :], pc("gla_g", hd), G_RS[:, hd % 2, :], ALU.mult, ALU.mult
                                       ).then_inc(g_t1, 1)
                v.wait_ge(g_t1, hd + 1)
                v.tensor_tensor(t, t, GR[:, hd, :], ALU.mult).then_inc(g_t2, 1)
                v.wait_ge(z_hi, 4 + hd + 1)
                v.tensor_tensor(zl[:, 4 + hd, :], t, zh[:, 4 + hd, :].bitcast(F), ALU.subtract).then_inc(z_lo, 1)

        GATE = arena[:, 0:16, :]
        BT = arena[:, 16:20, :]
        BY = arena[:, 20:22, :]
        gate_pre, gate_done = sem("gate_pre"), sem("gate_done")
        br_t, br_y, br_hi = sem("br_t"), sem("br_y"), sem("br_hi")

        def gates_dve(v):
            def body(c, slot, l):
                v.wait_ge(mm_done, c + 1)
                for m in range(2):
                    ins = v.tensor_scalar(GATE[:, bass.ds(l * 2 + m, 1), :], pairs[:, 2 * slot + m:2 * slot + m + 1, :],
                                          pc_at("b_gate", l * 2 + m), None, ALU.add)
                ins.then_inc(drained, 1)
            chunk_loop(v, "gates", body)

        def gates_act(a):
            def body(c, slot, l):
                hi_part(a, c + 1, 1 - slot)
                a.wait_ge(drained, c + 1)
                a.wait_ge(consts, 32)
                tile = GATE[:, bass.ds(l * 2, 2), :]
                a.activation(tile, tile, ACT.Sigmoid).then_inc(gate_done, 1)
            chunk_loop(a, "gates", body)

        def branch_dve(v):
            v.wait_ge(gate_done, COUNT["gates"])

            def body(c, slot, l):
                v.wait_ge(mm_done, c + 1)
                for b in range(2):
                    v.tensor_tensor(BT[:, 2 * slot + b:2 * slot + b + 1, :], GATE[:, bass.ds(l + 8 * b, 1), :],
                                    pairs[:, 2 * slot + b:2 * slot + b + 1, :], ALU.mult).then_inc(br_t, 1)
                v.wait_ge(br_t, l * 2 + 2)
                v.tensor_tensor(BY[:, slot, :], BT[:, 2 * slot, :], BT[:, 2 * slot + 1, :], ALU.add).then_inc(br_y, 1)
                v.wait_ge(br_hi, l + 1)
                v.tensor_tensor(xl[:, bass.ds(l, 1), :], BY[:, slot:slot + 1, :], xh[:, bass.ds(l, 1), :].bitcast(F),
                                ALU.subtract).then_inc(drained, 1)
            chunk_loop(v, "branch", body)

        def branch_act(a):
            def body(c, slot, l):
                hi_part(a, c + 1, 1 - slot)
                a.wait_ge(br_y, l + 1)
                a.wait_ge(consts, 32)
                a.activation(xh[:, bass.ds(l, 1), :], BY[:, slot:slot + 1, :], ACT.Copy).then_inc(br_hi, 1)
            chunk_loop(a, "branch", body)

        UW = T + 2 * PAD
        UP = arena[:, 0:5, :].rearrange("p a b -> p (a b)")[:, 0:4 * UW].rearrange("p (g u) -> p g u", u=UW)
        AQ = arena[:, 5:9, :]
        AKD = arena[:, 9:11, :]
        AV = arena[:, 11, :].rearrange("p (b n) -> p b n", n=P)
        ROPE = arena[:, 12:14, :]
        WPOOL = arena[:, 14, :]
        AP_ = arena[:, 15:17, :]
        APT = arena[:, 17:21, :]
        AK = arena[:, 21, :]
        A_SQ, A_RS, A_QN = arena[:, 22, :], arena[:, 23, :], arena[:, 24, :]
        A_T1, A_T2 = arena[:, 25, :], arena[:, 26, :]
        POOLC = arena[:, 17:22, :]
        PW = [arena[:, 22:24, :].rearrange("p a b -> p (a b)"), arena[:, 24:26, :].rearrange("p a b -> p (a b)")]
        pool_in, rope_in = sem("pool_in"), sem("rope_in")
        u_zero, u_step, u_pooled, u_mm, u_out = (sem("u_zero"), sem("u_step"), sem("u_pooled"), sem("u_mm"),
                                                 sem("u_out"))
        POOL_STEPS = [3, 4, 5, 6]

        def pool_dve(v):
            v.wait_ge(pool_in, 16)
            done = 0
            v.tensor_copy(WPOOL, POOLC[:, 4, :]).then_inc(u_step, 1)
            done += 1
            for g in range(4):
                src = UP[:, g, :]
                size = UW
                if g:
                    v.wait_ge(u_pooled, g)
                for lev in range(g + 1):
                    step = 1 << lev
                    size -= step
                    dst = PW[lev % 2][:, 0:size]
                    v.wait_ge(u_step, done)
                    v.tensor_tensor(dst, src[:, 0:size], src[:, step:step + size], ALU.add).then_inc(u_step, 1)
                    done += 1
                    src = dst
                at = PAD - (1 << g)
                v.wait_ge(u_step, done)
                v.tensor_tensor(PW[(g + 1) % 2][:, 0:T], src[:, at:at + T], POOLC[:, g, :], ALU.mult
                                ).then_inc(u_step, 1)
                done += 1
                v.wait_ge(u_step, done)
                own = UP[:, g, PAD:PAD + T]
                v.tensor_tensor(own, PW[(g + 1) % 2][:, 0:T], own, ALU.subtract).then_inc(u_pooled, 1)

        def pool_pe(p):
            p.wait_ge(u_pooled, 4)
            for g in range(4):
                p.matmul(aux[:, g, :], WPOOL[:, g * P:(g + 1) * P], UP[:, g, PAD:PAD + T], start=True, stop=True
                         ).then_inc(u_mm, 1)

        def pool_out_dve(v):
            for g in range(5):
                if g < 4:
                    v.wait_ge(u_mm, g + 1)
                    v.tensor_scalar(UP[:, g, PAD:PAD + T], aux[:, g, :], pc("b_pool", g), pc("pool_scale", g),
                                    ALU.add, ALU.mult).then_inc(u_out, 1)
                if g:
                    v.wait_ge(z_hi, 8 + g)
                    v.tensor_tensor(zl[:, g - 1, :], UP[:, g - 1, PAD:PAD + T], zh[:, g - 1, :].bitcast(F),
                                    ALU.subtract).then_inc(z_lo, 1)

        def pool_out_act(a):
            for g in range(4):
                a.wait_ge(u_out, g + 1)
                a.activation(zh[:, g, :], UP[:, g, PAD:PAD + T], ACT.Copy).then_inc(z_hi, 1)

        r_sq, r_ms, r_ln, r_rs, r_qn = sem("r_sq"), sem("r_ms"), sem("r_ln"), sem("r_rs"), sem("r_qn")
        r_rot, r_t1, r_t2, r_out = sem("r_rot"), sem("r_t1"), sem("r_t2"), sem("r_out")
        e_z, e_max, e_p, e_rc, e_pn = sem("e_z"), sem("e_max"), sem("e_p"), sem("e_rc"), sem("e_pn")
        e_t, e_tc, e_pv = sem("e_t"), sem("e_tc"), sem("e_pv")
        A_MAX, A_SUM, A_RC = small[:, 0:32], small[:, 32:64], small[:, 64:96]
        AN = ATT_H * TB

        def rope_src(x):
            return AQ[:, x, :] if x < 4 else AK

        def att_pe(p):
            p.wait_ge(u_out, 4)
            for x in range(5):
                p.wait_ge(r_sq, x + 1)
                if x:
                    p.wait_ge(r_ln, x)
                p.matmul(aux[:, 0, :], cm("bd64"), A_SQ, start=True, stop=True).then_inc(r_ms, 1)
                p.wait_ge(r_qn, x + 1)
                if x:
                    p.wait_ge(r_t2, x)
                p.matmul(aux[:, 1, :], cm("rot"), A_QN, start=True, stop=True).then_inc(r_rot, 1)
            p.wait_ge(r_out, 5)

            def scores(n):
                hd, tb = n // TB, n % TB
                r = (hd % 2) * 64
                if n >= 2:
                    p.wait_ge(e_p, n - 1)
                p.matmul(aux[:, n % 2, :], AQ[r:r + 64, hd // 2, tb * P:(tb + 1) * P],
                         AKD[r:r + 64, hd // 4, :], start=True, stop=True).then_inc(e_z, 1)

            def turn(n):
                p.wait_ge(e_pn, n + 1)
                if n:
                    p.wait_ge(e_tc, n)
                for sb_ in range(TB):
                    mm = p.transpose(aux[:, 2, sb_ * P:(sb_ + 1) * P], AP_[:, n % 2, sb_ * P:(sb_ + 1) * P],
                                     cm("ident"))
                mm.then_inc(e_t, 1)

            def values(hd):
                r = (hd % 2) * 64
                p.wait_ge(e_tc, TB * (hd + 1))
                if hd % 2 == 0 and hd:
                    p.wait_ge(z_lo, 12 + hd // 2)
                for sb_ in range(TB):
                    mm = p.matmul(aux[r:r + 64, 3, :], AV[:, sb_, (hd // 4) * 64:(hd // 4) * 64 + 64], APT[:, sb_, :],
                                  start=(sb_ == 0), stop=(sb_ == TB - 1))
                mm.then_inc(e_pv, 1)

            scores(0)
            scores(1)
            for n in range(AN):
                turn(n)
                if n + 2 < AN:
                    scores(n + 2)
                if n % TB == TB - 1:
                    values(n // TB)

        def att_act(a):
            for x in range(5):
                if x == 0:
                    a.wait_ge(drained, end_of("att_kv"))
                else:
                    a.wait_ge(r_ms, x)
                a.activation(A_SQ, rope_src(x), ACT.Square).then_inc(r_sq, 1)
                a.wait_ge(r_ms, x + 1)
                if x:
                    a.wait_ge(r_qn, x)
                a.activation(A_RS, aux[:, 0, :], ACT.Ln, scale=1.0 / 64, bias=pc("eps")).then_inc(r_ln, 1)
                a.wait_ge(r_ln, x + 1)
                a.activation(A_RS, A_RS, ACT.Exp, scale=-0.5).then_inc(r_rs, 1)

            def copy_t(n):
                a.wait_ge(e_t, n + 1)
                if n % TB == 0 and n:
                    a.wait_ge(e_pv, n // TB)
                tb = n % TB
                a.activation(APT[:, :, tb * P:(tb + 1) * P], aux[:, 2, :].rearrange("p (s t) -> p s t", t=P),
                             ACT.Copy).then_inc(e_tc, 1)

            def out_hi(pr):
                a.wait_ge(e_pv, 2 * (pr + 1))
                a.activation(zh[:, 4 + pr, :], aux[:, 3, :], ACT.Copy).then_inc(z_hi, 1)

            for n in range(AN):
                a.wait_ge(e_max, n + 1)
                if n >= 2:
                    a.wait_ge(e_t, n - 1)
                a.activation(AP_[:, n % 2, :], aux[:, n % 2, :], ACT.Exp, bias=A_MAX[:, n:n + 1],
                             accum_out=A_SUM[:, n:n + 1]).then_inc(e_p, 1)
                if n:
                    copy_t(n - 1)
                if n % (2 * TB) == 1 and n > 1:
                    out_hi(n // (2 * TB) - 1)
            copy_t(AN - 1)
            out_hi(ATT_H // 2 - 1)

        def att_dve(v):
            v.wait_ge(rope_in, 16)
            for x in range(5):
                v.wait_ge(r_rs, x + 1)
                if x:
                    v.wait_ge(r_rot, x)
                v.scalar_tensor_tensor(A_QN, rope_src(x), pc("q_gain" if x < 4 else "k_gain"), A_RS,
                                       ALU.mult, ALU.mult).then_inc(r_qn, 1)
                v.wait_ge(r_qn, x + 1)
                if x:
                    v.wait_ge(r_out, x)
                by = 1.0 if x < 4 else SB_D ** -0.5
                v.scalar_tensor_tensor(A_T1, A_QN, by, ROPE[:, 0, :], ALU.mult, ALU.mult).then_inc(r_t1, 1)
                v.wait_ge(r_rot, x + 1)
                v.scalar_tensor_tensor(A_T2, aux[:, 1, :], by, ROPE[:, 1, :], ALU.mult, ALU.mult).then_inc(r_t2, 1)
                v.wait_ge(r_t1, x + 1)
                v.wait_ge(r_t2, x + 1)
                if x < 4:
                    v.tensor_tensor(AQ[:, x, :], A_T1, A_T2, ALU.add).then_inc(r_out, 1)
                else:
                    for kv in range(2):
                        for r in (0, 64):
                            ins = v.tensor_tensor(AKD[r:r + 64, kv, :], A_T1[kv * 64:kv * 64 + 64, :],
                                                  A_T2[kv * 64:kv * 64 + 64, :], ALU.add)
                    ins.then_inc(r_out, 1)

            def out_lo(pr):
                v.wait_ge(z_hi, 12 + pr + 1)
                v.tensor_tensor(zl[:, 4 + pr, :], aux[:, 3, :], zh[:, 4 + pr, :].bitcast(F), ALU.subtract
                                ).then_inc(z_lo, 1)

            def row_max(n):
                v.wait_ge(e_z, n + 1)
                v.tensor_reduce(A_MAX[:, n:n + 1], aux[:, n % 2, :], AX_X, ALU.max, negate=True).then_inc(e_max, 1)

            row_max(0)
            for n in range(AN):
                if n + 1 < AN:
                    row_max(n + 1)
                v.wait_ge(e_p, n + 1)
                v.reciprocal(A_RC[:, n:n + 1], A_SUM[:, n:n + 1]).then_inc(e_rc, 1)
                v.wait_ge(e_rc, n + 1)
                v.tensor_scalar(AP_[:, n % 2, :], AP_[:, n % 2, :], A_RC[:, n:n + 1], None, ALU.mult).then_inc(e_pn, 1)
                if n % (2 * TB) == 2 and n > 2:
                    out_lo(n // (2 * TB) - 1)
            out_lo(ATT_H // 2 - 1)

        MV = arena[:, 0:8, :].rearrange("p (b x) n -> p b (x n)", b=TB)
        MQK = arena[:, 8:16, :]
        CPAD = [arena[:, 16 + 2 * i:18 + 2 * i, :].rearrange("p a b -> p (a b)")[:, 0:T + 4] for i in range(4)]
        CO = arena[:, 24:28, :]
        m_zero, m_conv, m_raw, m_silu = sem("m_zero"), sem("m_conv"), sem("m_raw"), sem("m_silu")

        def conv5_dve(v):
            for i in range(4):
                ins = v.memset(CPAD[i][:, 0:2], 0.0)
                ins = v.memset(CPAD[i][:, T + 2:T + 4], 0.0)
            ins.then_inc(m_zero, 1)
            v.wait_ge(m_zero, 1)

            def body(c, slot, l):
                v.wait_ge(mm_done, c + 1)
                v.wait_ge(m_conv, l * 10)
                pads = arena[:, 16 + 4 * slot:20 + 4 * slot, :].rearrange("p (m a) b -> p m (a b)", m=2)
                v.tensor_scalar(pads[:, :, 2:T + 2], pairs[:, 2 * slot:2 * slot + 2, :], 1.0, None, ALU.mult
                                ).then_inc(drained, 1)
                v.wait_ge(drained, c + 1)
                for m in range(2):
                    pad = pads[:, m, :]
                    at = l * 2 + m
                    dst = CO[:, 2 * slot + m, :]
                    w = lambda tap: pc_at("od_conv_w", at + tap * 8)
                    v.tensor_scalar(dst, pad[:, 0:T], w(0), pc_at("od_conv_b", at), ALU.mult, ALU.add
                                    ).then_inc(m_conv, 1)
                    for tap in range(1, 5):
                        v.wait_ge(m_conv, l * 10 + (5 * m + tap))
                        out = dst if tap < 4 else MQK[:, bass.ds(at, 1), :]
                        src0, src1 = pad[:, tap:tap + T], dst
                        if tap == 4:
                            src0 = pads[:, m:m + 1, tap:tap + T]
                            src1 = CO[:, 2 * slot + m:2 * slot + m + 1, :]
                        v.scalar_tensor_tensor(out, src0, w(tap), src1, ALU.mult, ALU.add).then_inc(m_conv, 1)
            chunk_loop(v, "ml_qk", body)

        GROW = 40
        rows = {name: arena[0:64, 16 + i, :] for i, name in enumerate(("gi", "gf", "cap", "sum", "u", "mx", "m"))}
        ONE_ROWS = arena[0:64, 23, :]
        M_UT = small[:, 0:4 * GROW].rearrange("p (b c) -> p b c", c=GROW)
        m_gate, m_fc, m_fe, m_fl, m_lf = sem("m_gate"), sem("m_fc"), sem("m_fe"), sem("m_fl"), sem("m_lf")
        m_b, m_u, m_mx, m_m, m_ut, m_utc = sem("m_b"), sem("m_u"), sem("m_mx"), sem("m_m"), sem("m_ut"), sem("m_utc")

        def gate_rows_dve(v):
            def body(c, slot, l):
                v.wait_ge(mm_done, c + 1)
                b = pairs[:, 2 * slot, :]
                v.tensor_scalar(rows["gi"][0:GROW, :], b[0:GROW, :], pc("gate_b", 0)[0:GROW], None, ALU.add
                                ).then_inc(m_gate, 1)
                v.tensor_scalar(rows["gf"][0:GROW, :], b[64:64 + GROW, :], pc("gate_b", 1)[64:64 + GROW], -1.0,
                                ALU.add, ALU.mult).then_inc(drained, 1)
            chunk_loop(v, "ml_g", body)

        def scans_dve(v):
            v.wait_ge(drained, end_of("ml_g"))
            r40 = lambda n: rows[n][0:GROW, :]
            v.memset(ONE_ROWS, 1.0).then_inc(m_zero, 1)
            v.tensor_scalar(r40("cap"), r40("gf"), SP_CAP, None, ALU.min).then_inc(m_fc, 1)
            v.wait_ge(m_fl, 1)
            v.tensor_tensor(r40("gf"), r40("gf"), r40("cap"), ALU.max).then_inc(m_lf, 1)
            v.wait_ge(m_lf, 1)
            v.wait_ge(m_zero, 2)
            v.memset(rows["sum"], 0.0).then_inc(m_b, 1)
            v.memset(rows["mx"], 0.0).then_inc(m_b, 1)
            v.wait_ge(m_b, 2)
            fwd, bwd = (slice(0, 8), slice(None)), (slice(32, 40), slice(None, None, -1))
            for d in (fwd, bwd):
                v.tensor_tensor_scan(rows["sum"][d], ONE_ROWS[d], rows["gf"][d], 0.0, ALU.mult, ALU.add
                                     ).then_inc(m_b, 1)
            v.wait_ge(m_b, 4)
            v.wait_ge(m_gate, 1)
            v.tensor_tensor(r40("u"), r40("gi"), r40("sum"), ALU.add).then_inc(m_u, 1)
            v.wait_ge(m_u, 1)
            for d in (fwd, bwd):
                v.tensor_tensor_scan(rows["mx"][d], rows["u"][d], rows["u"][d], 0.0, ALU.max, ALU.max
                                     ).then_inc(m_mx, 1)
            v.wait_ge(m_mx, 2)
            v.tensor_tensor(r40("m"), r40("mx"), r40("sum"), ALU.subtract).then_inc(m_m, 1)
            v.wait_ge(m_m, 1)
            v.tensor_scalar(r40("mx"), r40("mx"), -1.0, None, ALU.mult).then_inc(m_m, 1)
            v.wait_ge(m_ut, 1)
            v.tensor_copy(M_UT, aux[:, 0, 0:4 * GROW].rearrange("p (b c) -> p b c", c=GROW)).then_inc(m_utc, 1)

        def scans_act(a):
            a.wait_ge(m_fc, 1)
            a.activation(rows["cap"][0:GROW, :], rows["cap"][0:GROW, :], ACT.Exp).then_inc(m_fe, 1)
            a.wait_ge(m_fe, 1)
            a.activation(rows["cap"][0:GROW, :], rows["cap"][0:GROW, :], ACT.Ln, bias=1.0).then_inc(m_fl, 1)

        def scans_pe(p):
            p.wait_ge(m_u, 1)
            for tb in range(TB):
                mm = p.transpose(aux[:, 0, tb * GROW:(tb + 1) * GROW], rows["u"][0:GROW, tb * P:(tb + 1) * P],
                                 cm("ident")[0:GROW, 0:GROW])
            mm.then_inc(m_ut, 1)

        ME = arena[:, 23:27, :]
        M_EM = arena[:, 16:18, :]
        M_DG = arena[:, 18, :]
        M_H = arena[:, 19:21, :]
        M_HS = arena[:, 27, :]
        M_HOLD = ada_acc[:, :, :].rearrange("p a b -> p (a b)")
        k_bcc, k_keep = sem("k_bcc"), sem("k_keep")
        k_bc, k_z, k_dg, k_e, k_s = sem("k_bc"), sem("k_z"), sem("k_dg"), sem("k_e"), sem("k_s")
        k_pv, k_em, k_emx, k_dm, k_ln, k_r = (sem("k_pv"), sem("k_em"), sem("k_emx"), sem("k_dm"), sem("k_ln"),
                                              sem("k_r"))
        k_h, k_hs, k_sq, k_ms, k_ml, k_mr, k_hn = (sem("k_h"), sem("k_hs"), sem("k_sq"), sem("k_ms"), sem("k_ml"),
                                                   sem("k_mr"), sem("k_hn"))

        def span(d, i):
            if d == 0:
                return (i * P, T), (i * P, (i + 1) * P), ((i + 1) * P, T)
            return (0, (i + 1) * P), (i * P, (i + 1) * P), (0, i * P)

        def pick(d, hd):
            row = hd + 32 * d
            return cm("ident")[0:GROW, row:row + 1].to_broadcast([GROW, P])

        def ml_pe(p):
            p.wait_ge(drained, end_of("ml_g"))
            p.wait_ge(m_utc, 1)
            p.wait_ge(m_silu, 1)
            p.wait_ge(m_m, 2)
            for hd in range(ML_H):
                r = (hd % 2) * 64
                if hd:
                    p.wait_ge(k_hn, hd)
                for d in range(2):
                    p.matmul(aux[:, 2 + d, :], pick(d, hd), rows["mx"][0:GROW, :], start=True, stop=True
                             ).then_inc(k_bc, 1)

                def score(i):
                    if i >= 2:
                        p.wait_ge(k_s, 8 * hd + 2 * (i - 1))
                    p.matmul(aux[:, i % 2, :], MQK[r:r + 64, 4 + hd // 2, i * P:(i + 1) * P],
                             MQK[r:r + 64, hd // 2, :], start=True, stop=True).then_inc(k_z, 1)
                score(0)
                score(1)
                for i in range(TB):
                    for d in range(2):
                        (lo, hi), _, _ = span(d, i)
                        p.wait_ge(k_s, 8 * hd + 2 * i + d + 1)
                        e = ME[:, 2 * d + i % 2, lo:hi]
                        p.matmul(pairs[:, d, lo:hi], MV[:, i, hd * P:(hd + 1) * P], e, start=(i == 0),
                                 stop=(i == TB - 1), skip_group_check=True)
                        p.matmul(pairs[:, 2 + d, lo:hi], cm("ones"), e, start=(i == 0), stop=(i == TB - 1),
                                 skip_group_check=True).then_inc(k_pv, 1)
                    if i + 2 < TB:
                        score(i + 2)
                for d in range(2):
                    p.wait_ge(k_s, 8 * (hd + 1))
                    p.matmul(aux[:, d, :], pick(d, hd), rows["m"][0:GROW, :], start=True, stop=True
                             ).then_inc(k_em, 1)
                p.wait_ge(k_sq, hd + 1)
                p.matmul(aux[:, 2, :], cm("ones"), M_HS, start=True, stop=True).then_inc(k_ms, 1)

        def ml_act(a):
            for hd in range(ML_H):
                for d in range(2):
                    a.wait_ge(k_bc, 2 * hd + d + 1)
                    if hd:
                        a.wait_ge(k_h, 2 * hd)
                    a.activation(M_EM[:, d, :], aux[:, 2 + d, :], ACT.Copy).then_inc(k_bcc, 1)
                for i in range(TB):
                    for d in range(2):
                        _, (dlo, dhi), (lo, hi) = span(d, i)
                        step = 8 * hd + 2 * i + d
                        e = ME[:, 2 * d + i % 2, :]
                        a.wait_ge(k_bcc, 2 * hd + d + 1)
                        a.wait_ge(m_utc, 1)
                        if step >= 4:
                            a.wait_ge(k_pv, step - 3)
                        if hi > lo:
                            a.activation(e[:, lo:hi], M_EM[:, d, lo:hi], ACT.Exp,
                                         bias=M_UT[:, i, hd + 32 * d:hd + 32 * d + 1])
                        a.wait_ge(k_dg, step + 1)
                        a.activation(e[:, dlo:dhi], M_DG[:, (step % 4) * P:(step % 4 + 1) * P], ACT.Exp
                                     ).then_inc(k_e, 1)
                for d in range(2):
                    a.wait_ge(k_em, 2 * hd + d + 1)
                    a.activation(M_EM[:, d, :], aux[:, d, :], ACT.Exp, scale=-1.0).then_inc(k_emx, 1)
                for d in range(2):
                    a.wait_ge(k_dm, 4 * hd + 2 * d + 2)
                    a.activation(M_EM[:, d, :], M_EM[:, d, :], ACT.Ln).then_inc(k_ln, 1)
                    a.wait_ge(k_ln, 2 * hd + d + 1)
                    a.activation(M_EM[:, d, :], M_EM[:, d, :], ACT.Exp, scale=-1.0).then_inc(k_r, 1)
                a.wait_ge(k_hs, hd + 1)
                a.activation(M_HS, M_H[:, 0, :], ACT.Square).then_inc(k_sq, 1)
                a.wait_ge(k_ms, hd + 1)
                a.activation(M_HS, aux[:, 2, :], ACT.Ln, scale=1.0 / P, bias=pc("eps")).then_inc(k_ml, 1)
                a.wait_ge(k_ml, hd + 1)
                a.activation(M_HS, M_HS, ACT.Exp, scale=-0.5).then_inc(k_mr, 1)

        def ml_dve(v):
            for hd in range(ML_H):
                def diag(i, d):
                    _, (lo, hi), _ = span(d, i)
                    step = 8 * hd + 2 * i + d
                    v.wait_ge(k_bcc, 2 * hd + d + 1)
                    if step >= 4:
                        v.wait_ge(k_e, step - 3)
                    v.scalar_tensor_tensor(M_DG[:, (step % 4) * P:(step % 4 + 1) * P], M_EM[:, d, lo:hi],
                                           M_UT[:, i, hd + 32 * d:hd + 32 * d + 1], cm("neg_fwd" if d == 0 else
                                                                                      "neg_bwd"),
                                           ALU.add, ALU.add).then_inc(k_dg, 1)
                for i in range(TB):
                    for d in range(2):
                        (lo, hi), _, _ = span(d, i)
                        step = 8 * hd + 2 * i + d
                        diag(i, d)
                        v.wait_ge(k_e, step + 1)
                        v.wait_ge(k_z, 4 * hd + i + 1)
                        e = ME[:, 2 * d + i % 2, lo:hi]
                        v.scalar_tensor_tensor(e, aux[:, i % 2, lo:hi], SB_D ** -0.5, e, ALU.mult, ALU.mult
                                               ).then_inc(k_s, 1)
                for d in range(2):
                    v.wait_ge(k_emx, 2 * hd + d + 1)
                    v.wait_ge(k_pv, 8 * hd + 7 + d)
                    den = pairs[:, 2 + d, :]
                    em = M_EM[:, d, :]
                    v.tensor_tensor(em, den, em, ALU.max).then_inc(k_dm, 1)
                    v.wait_ge(k_dm, 4 * hd + 2 * d + 1)
                    v.scalar_tensor_tensor(em, den, -1.0, em, ALU.mult, ALU.max).then_inc(k_dm, 1)
                for d in range(2):
                    v.wait_ge(k_r, 2 * hd + d + 1)
                    v.tensor_tensor(M_H[:, d, :], pairs[:, d, :], M_EM[:, d, :], ALU.mult).then_inc(k_h, 1)
                v.wait_ge(k_h, 2 * hd + 2)
                v.tensor_tensor(M_H[:, 0, :], M_H[:, 0, :], M_H[:, 1, :], ALU.add).then_inc(k_hs, 1)
                v.wait_ge(k_mr, hd + 1)
                if hd % 2 == 0 and hd:
                    v.wait_ge(k_keep, hd // 2)
                dst = MQK[:, 4 + hd // 2, :] if hd % 2 else M_HOLD
                v.scalar_tensor_tensor(dst, M_H[:, 0, :], pc("head_gain", hd), M_HS, ALU.mult, ALU.mult
                                       ).then_inc(k_hn, 1)
                if hd % 2:
                    v.tensor_copy(MQK[:, hd // 2, :], M_HOLD).then_inc(k_keep, 1)

        OSIG = arena[:, 16:20, :]
        OV = arena[:, 20:24, :]
        o_sig, o_val = sem("o_sig"), sem("o_val")

        def ml_o_act(a):
            def body(c, slot, l):
                hi_part(a, c + 1, 1 - slot)
                a.wait_ge(mm_done, c + 1)
                a.activation(OSIG[:, 2 * slot:2 * slot + 2, :], pairs[:, 2 * slot:2 * slot + 2, :], ACT.Sigmoid
                             ).then_inc(o_sig, 1)
                a.wait_ge(o_val, l + 1)
                a.wait_ge(consts, 32)
                a.activation(zh[:, bass.ds(l * 2, 2), :], OV[:, 2 * slot:2 * slot + 2, :], ACT.Copy).then_inc(z_hi, 1)
            chunk_loop(a, "ml_o", body)

        def ml_o_dve(v):
            v.wait_ge(k_keep, ML_H // 2)

            def body(c, slot, l):
                v.wait_ge(o_sig, l + 1)
                for m in range(2):
                    ins = v.tensor_tensor(OV[:, 2 * slot + m:2 * slot + m + 1, :], MQK[:, bass.ds(l + 4 * m, 1), :],
                                          OSIG[:, 2 * slot + m:2 * slot + m + 1, :], ALU.mult)
                ins.then_inc(o_val, 1)
                v.wait_ge(z_hi, l + (16 + 1))
                v.tensor_tensor(zl[:, bass.ds(l * 2, 2), :], OV[:, 2 * slot:2 * slot + 2, :],
                                zh[:, bass.ds(l * 2, 2), :].bitcast(F), ALU.subtract).then_inc(drained, 1)
            chunk_loop(v, "ml_o", body)

        block = ctx.enter_context(nc.Block())
        streams = {2048: w2048, 1024: w1024, HALF * P: w1408}

        def x_split(n):
            return (x_ready, KT * n)

        def gate_col(layer, base):
            return lambda i: mod[:, layer, bass.ds(i + base, 1)]

        @block.sync
        def _(sp):
            sp.dma_start(h[:, :, :], xT.rearrange("p (k t) -> p k t", t=T)).then_inc(x_in, 16)
            sp.dma_start(par[:, :], par_d).then_inc(consts, 16)
            sp.dma_start(cst[:, :], cst_d).then_inc(consts, 16)
            sp.dma_start(G_CST[:, 0:GLA_W], gla_d).then_inc(gla_in, 16)
            for stage, kind, _ in STAGES:
                w = WIDTH[kind]
                if stage in ("up0", "e_up0"):
                    layer = 0 if stage == "up0" else 1
                    if layer == 0:
                        sp.wait_ge(drained, end_of("branch"))
                    else:
                        sp.wait_ge(z_lo, 16)
                    for A in (ADA_N * layer, ADA_N * layer + 1):
                        ada_load(sp, A, A % 2)

                def body(c, slot, l):
                    if not (is_static(c) and c < 2):
                        sp.wait_ge(lo_done, c - 1)
                    sp.dma_start(raw[:, slot, 0:w], streams[w][bass.ds(l + ROW0[stage], 1), :, :]
                                 .rearrange("a p n -> p (a n)")).then_inc(raw_full[slot], 16)
                    if stage in ADA_OF:
                        ada_load(sp, l + ADA_OF[stage], ada_slot(stage, slot))
                chunk_loop(sp, stage, body)
            for k in range(KT):
                sp.wait_ge(drained, C0["o_down1"] + k + 1)
                sp.dma_start(outT[:, k * T:(k + 1) * T], h[:, k, :]).then_inc(stored, 16)
            sp.wait_ge(stored, 16 * KT)

        @block.gpsimd
        def _(g):
            for stage, kind, _ in STAGES:
                w = WIDTH[kind]

                def body(c, slot, l):
                    g.wait_ge(hi_done, c + 1)
                    g.tensor_tensor(wl[:, slot, 0:w], raw[:, slot, 0:w], wh[:, slot, 0:w].bitcast(F), ALU.subtract
                                    ).then_inc(lo_done, 1)
                chunk_loop(g, stage, body)

        @block.scalar
        def _(a):
            hi_part(a, 0, 0)
            a.wait_ge(consts, 32)
            a.activation(cond[:, :], pc("c", 0, KT), ACT.Silu).then_inc(s("cond_done"), 1)
            norm_act(a, "n_mix")
            for stage in ("sb_q", "sb_k", "sb_v"):
                hi_only(a, stage)
            sb_act(a)
            for stage in ("g_q", "g_k", "g_v", "g_r", "g_a"):
                hi_only(a, stage)
            gla_act(a)
            gates_act(a)
            branch_act(a)
            hi_only(a, "out")
            norm_act(a, "n_ffn")
            for i in range(2):
                up_act(a, f"up{i}")
                hi_only(a, f"down{i}")
            a.wait_ge(drained, end_of("up1"))
            a.dma_start(ROPE[:, :, :], rope_d.rearrange("p (a t) -> p a t", t=T)).then_inc(rope_in, 16)
            a.dma_start(POOLC[:, :, :], pool_d.rearrange("p (a t) -> p a t", t=T)).then_inc(pool_in, 16)
            norm_act(a, "n_final")
            norm_act(a, "n_e1")
            for stage in ("pool_u", "att_q", "att_kv"):
                hi_only(a, stage)
            pool_out_act(a)
            att_act(a)
            hi_only(a, "att_out")
            norm_act(a, "n_e2")
            for i in range(2):
                up_act(a, f"e_up{i}")
                hi_only(a, f"e_down{i}")
            norm_act(a, "n_o1")
            hi_only(a, "ml_qk")
            a.wait_ge(m_conv, 40)
            a.activation(MQK, MQK, ACT.Silu).then_inc(m_silu, 1)
            for stage in ("ml_v", "ml_g"):
                hi_only(a, stage)
            a.preload_act_table_set("natural_log_exp_and_others")
            scans_act(a)
            ml_act(a)
            ml_o_act(a)
            hi_only(a, "ml_out")
            norm_act(a, "n_o2")
            for i in range(2):
                up_act(a, f"o_up{i}")
                hi_only(a, f"o_down{i}")

        @block.vector
        def _(v):
            norm_dve(v, "n_mix")
            drain_copy(v, "sb_q", lambda l: SBQ[:, bass.ds(l * 2, 2), :], SB_D ** -0.5)
            drain_copy(v, "sb_k", lambda l: SBK[:, bass.ds(l * 2, 2), :])
            drain_copy(v, "sb_v", lambda l: SBV[:, :, bass.ds(l * 256, 256)])
            sb_dve(v)
            drain_copy(v, "g_q", lambda l: GQ, SB_D ** -0.5)
            drain_copy(v, "g_k", lambda l: GK)
            drain_copy(v, "g_v", lambda l: GV[:, :, bass.ds(l * 256, 256)])
            drain_copy(v, "g_r", lambda l: GR[:, bass.ds(l * 2, 2), :])

            def low_rank(c, slot, l):
                v.wait_ge(mm_done, c + 1)
                v.tensor_copy(G_A[0:16, :], pairs[0:16, 2 * slot, :]).then_inc(drained, 1)
            chunk_loop(v, "g_a", low_rank)
            gla_dve(v)
            gates_dve(v)
            branch_dve(v)
            drain_residual(v, "out")
            norm_dve(v, "n_ffn")
            for i in range(2):
                ins = v.memset(apad[i][:, 0:2], 0.0)
            ins.then_inc(s("pad_zero"), 1)
            v.wait_ge(s("pad_zero"), 1)
            v.wait_ge(s("cond_done"), 1)
            for A in range(2):
                ada_dve(v, A, A)
            for i in range(2):
                up_dve(v, f"up{i}")
                drain_residual(v, f"down{i}")
            mod_dve(v, 0)
            norm_dve(v, "n_final")
            v.wait_ge(mod_done, 2)
            norm_dve(v, "n_e1")
            v.wait_ge(x_ready, KT * 3)
            v.memset(UP[:, :, 0:PAD], 0.0)
            v.memset(UP[:, :, PAD + T:UW], 0.0).then_inc(u_zero, 1)
            v.wait_ge(u_zero, 1)
            drain_copy(v, "pool_u", lambda l: UP[:, bass.ds(l * 2, 2), PAD:PAD + T])
            v.wait_ge(drained, end_of("pool_u"))
            pool_dve(v)
            drain_copy(v, "att_q", lambda l: AQ[:, bass.ds(l * 2, 2), :])

            def kv(c, slot, l):
                v.wait_ge(mm_done, c + 1)
                v.tensor_copy(AK, pairs[:, 2 * slot, :])
                v.tensor_copy(AV, pairs[:, 2 * slot + 1, :].rearrange("p (b n) -> p b n", n=P)).then_inc(drained, 1)
            chunk_loop(v, "att_kv", kv)
            pool_out_dve(v)
            att_dve(v)
            drain_residual(v, "att_out", gate_col(0, 16))
            norm_dve(v, "n_e2")
            for A in (ADA_N, ADA_N + 1):
                ada_dve(v, A, A % 2)
            for i in range(2):
                up_dve(v, f"e_up{i}")
                drain_residual(v, f"e_down{i}", gate_col(0, 40))
            mod_dve(v, 1)
            v.wait_ge(mod_done, 4)
            norm_dve(v, "n_o1")
            conv5_dve(v)
            drain_copy(v, "ml_v", lambda l: MV[:, :, bass.ds(l * 256, 256)])
            gate_rows_dve(v)
            scans_dve(v)
            ml_dve(v)
            ml_o_dve(v)
            drain_residual(v, "ml_out", gate_col(1, 16))
            norm_dve(v, "n_o2")
            for i in range(2):
                up_dve(v, f"o_up{i}")
                drain_residual(v, f"o_down{i}", gate_col(1, 40))

        @block.tensor
        def _(p):
            norm_pe(p, "n_mix")
            linear_pe(p, "sb_q", x_split(1))
            linear_pe(p, "sb_k")
            linear_pe(p, "sb_v")
            sb_pe(p)
            for stage in ("g_q", "g_k", "g_v", "g_r", "g_a"):
                linear_pe(p, stage)
            gla_pe(p)
            linear_pe(p, "gates")
            linear_pe(p, "branch", (z_lo, 8))
            linear_pe(p, "out", (drained, end_of("branch")))
            norm_pe(p, "n_ffn")
            for A in range(2):
                ada_pe(p, A, A, 0)
            for i in range(2):
                linear_pe(p, f"up{i}", x_split(2))
                linear_pe(p, f"down{i}", (drained, end_of(f"up{i}")))
            norm_pe(p, "n_final")
            norm_pe(p, "n_e1")
            linear_pe(p, "pool_u", x_split(3))
            linear_pe(p, "att_q")
            linear_pe(p, "att_kv")
            pool_pe(p)
            att_pe(p)
            linear_pe(p, "att_out", (z_lo, 16))
            norm_pe(p, "n_e2")
            for A in (ADA_N, ADA_N + 1):
                ada_pe(p, A, A % 2, 1)
            for i in range(2):
                linear_pe(p, f"e_up{i}", x_split(4))
                linear_pe(p, f"e_down{i}", (drained, end_of(f"e_up{i}")))
            norm_pe(p, "n_o1")
            linear_pe(p, "ml_qk", x_split(5))
            linear_pe(p, "ml_v")
            linear_pe(p, "ml_g")
            scans_pe(p)
            ml_pe(p)
            p.wait_ge(k_hn, ML_H)
            linear_pe(p, "ml_o")
            linear_pe(p, "ml_out", (drained, end_of("ml_o")))
            norm_pe(p, "n_o2")
            for i in range(2):
                linear_pe(p, f"o_up{i}", x_split(6))
                linear_pe(p, f"o_down{i}", (drained, end_of(f"o_up{i}")))


def chunks_of(w, cols):
    k, n = w.shape
    return np.ascontiguousarray(w.reshape(k // P, P, n // cols, cols).transpose(2, 1, 0, 3)).reshape(
        n // cols, P, k // P * cols)


def constant_matrices():
    r = np.arange(P)
    s_, t_ = r[:, None], r[None, :]
    rot = np.zeros((P, P), np.float32)
    rot[r[1::2], r[0::2]] = -1.0
    rot[r[0::2], r[1::2]] = 1.0
    mats = {
        "ident": s_ == t_, "ntri": -1.0 * (s_ >= t_), "ones": np.ones((P, P)), "nones": -np.ones((P, P)),
        "neg_strict": NEG * (s_ >= t_), "keep_strict": s_ < t_,
        "gla_mask": (s_ <= t_) & (s_ // GLA_C == t_ // GLA_C), "bd64": s_ // 64 == t_ // 64, "rot": rot,
        "neg_fwd": NEG * (s_ > t_), "neg_bwd": NEG * (s_ < t_),
    }
    return np.concatenate([np.asarray(mats[n], np.float32) for n in CST_COLS], axis=1)


def rope_tables():
    t = np.arange(T)
    inv = np.float32(10000.0) ** (-np.arange(16, dtype=np.float32) / np.float32(16))
    ang = np.concatenate([(t // 64).astype(np.float32)[:, None] * inv, (t % 64).astype(np.float32)[:, None] * inv],
                         axis=1)
    rows = [np.tile(np.repeat(f(ang).T, 2, axis=0), (2, 1)) for f in (np.cos, np.sin)]
    return np.concatenate(rows, axis=1).astype(np.float32)


def pool_reciprocals():
    t = np.arange(T)
    rows = []
    for w in (2, 4, 8, 16):
        lo, hi = np.clip(t - w // 2, 0, T), np.clip(t + w - w // 2, 0, T)
        rows.append(np.float32(1.0) / (hi - lo).astype(np.float32))
    return np.broadcast_to(np.concatenate(rows)[None], (P, 4 * T)).astype(np.float32)


def lay_out(i):
    f32 = np.float32
    w_in = i["w_in"][0]
    at = np.cumsum([0, 512, 512, 512, 256, 256, 512, 512, 16, 1024, 1024])
    cut = lambda n: w_in[:, at[n]:at[n + 1]]

    def pad_cols(w, places):
        out = np.zeros((w.shape[0], P), f32)
        for (a, b), place in places:
            out[:, place:place + b - a] = w[:, a:b]
        return out

    def paired(a, g):
        k = a.shape[0]
        return np.concatenate([a.reshape(k, -1, 1, P), g.reshape(k, -1, 1, P)], axis=2).reshape(k, -1)

    od = i["od_w_in_2"][0]
    ev = i["ev_w_in_2"][0]
    gate_places = [((0, 8), 0), ((16, 24), 32), ((8, 16), 64), ((24, 32), 96)]
    half = HALF * P
    s = {
        "sb_q": cut(0), "sb_k": cut(1), "sb_v": cut(2), "g_q": cut(3), "g_k": cut(4), "g_v": cut(5), "g_r": cut(6),
        "g_a": pad_cols(cut(7), [((0, 16), 0)]), "gates": w_in[:, at[8]:at[10]],
        "branch": np.concatenate([i["w_branch_sb"][0], i["w_branch_gla"][0]]), "out": i["w_out"][0],
        "pool_u": ev[:, 0:512], "att_q": ev[:, 512:1024], "att_kv": ev[:, 1024:1280], "att_out": i["ev_w_out_2"][0],
        "ml_qk": od[:, 0:1024], "ml_v": od[:, 1024:2048], "ml_o": od[:, 2048:3072],
        "ml_g": pad_cols(od[:, 3072:3104], gate_places), "ml_out": i["od_w_out_2"][0],
    }
    ffns = (("", i["w_ffn_in"][0][:, :FF], i["w_ffn_in"][0][:, FF:], i["w_ffn_out"][0]),
            ("e_", i["ffn_w1_2"][0], i["ffn_w3_2"][0], i["ffn_w2_2"][0]),
            ("o_", i["ffn_w1_2"][1], i["ffn_w3_2"][1], i["ffn_w2_2"][1]))
    for pre, wa, wg, wo in ffns:
        for n in range(2):
            c = slice(n * half, (n + 1) * half)
            s[f"{pre}up{n}"] = paired(wa[:, c], wg[:, c])
            s[f"{pre}down{n}"] = wo[c]
    streams = {}
    for name, kind, count in STAGES:
        ch = chunks_of(s[name], 256 if WIDTH[kind] == 2048 else P)
        streams.setdefault(WIDTH[kind], []).append(ch)
    col = lambda v: np.asarray(v, f32).reshape(-1, P).T
    gate_b = np.zeros((P, 2), f32)
    gb = i["od_gate_b_2"][0]
    for (a, b), place in gate_places:
        gate_b[place:place + b - a, place // 64] = gb[a:b]
    par = {
        "norm_mix": col(i["norm_mix_g"][0]), "b_gate": col(i["b_gate"][0]), "b_alpha": col(i["b_alpha"][0]),
        "gla_g": col(i["gla_norm_g"][0]), "norm_ffn": col(i["norm_ffn_g"][0]), "conv_w": col(i["conv_w"][0]),
        "conv_b": col(i["conv_b"][0]), "norm_final": col(i["norm_final_g"]), "c": col(i["c_2"][0]),
        "ada_b": col(i["ada_b_2"]), "b_pool": col(i["ev_b_pool_2"][0]), "pool_scale": col(i["ev_pool_scale_2"][0]),
        "q_gain": np.tile(i["ev_q_gain_2"][0], 2)[:, None], "k_gain": np.tile(i["ev_k_gain_2"][0], 2)[:, None],
        "od_conv_w": col(i["od_conv_w_2"][0]), "od_conv_b": col(i["od_conv_b_2"][0]), "gate_b": gate_b,
        "head_gain": col(i["od_head_gain_2"][0]), "eps": np.full((P, 1), EPS, f32),
    }
    reset = np.broadcast_to((np.arange(T) % GLA_C != 0).astype(f32)[None], (P, T))
    alpha = np.zeros((P, 256), f32)
    alpha[0:16] = i["w_alpha_up"][0]
    w_pool = i["ev_w_pool_2"][0].transpose(1, 0, 2).reshape(P, 4 * P)
    cat = lambda xs: np.ascontiguousarray(np.concatenate(xs, axis=1), dtype=f32)
    arrays = {
        "xT": np.ascontiguousarray(i["x"][0].T.reshape(KT, P, T).transpose(1, 0, 2)).reshape(P, KT * T),
        "w2048": np.concatenate(streams[2048]), "w1024": np.concatenate(streams[1024]),
        "w1408": np.concatenate(streams[HALF * P]),
        "ada": np.concatenate([chunks_of(i["ada_w_2"][n], 256) for n in range(2)]),
        "par": cat([par[n] for n in PAR_COLS]), "cst": constant_matrices(), "gla": cat([reset, alpha]),
        "rope": rope_tables(), "pool": cat([pool_reciprocals(), w_pool]),
    }
    return {f"in_{name}": a for name, a in arrays.items()}


def kernel(**inputs):
    import concourse.bacc as bacc
    from concourse.bass_utils import run_bass_kernel_spmd

    nc = bacc.Bacc("TRN2", target_bir_lowering=False, num_devices=1)
    arrays = lay_out({k: np.asarray(v) for k, v in inputs.items()})
    aps = [nc.dram_tensor(n, a.shape, F, kind="ExternalInput").ap() for n, a in arrays.items()]
    out = nc.dram_tensor("outT", (P, KT * T), F, kind="ExternalOutput").ap()
    build(nc, *aps, out)
    r = run_bass_kernel_spmd(nc, [arrays], core_ids=[0])
    got = r.results[0]["outT"]
    return np.ascontiguousarray(got.reshape(P, KT, T).transpose(2, 1, 0)).reshape(1, T, D)
```

```python
from contextlib import ExitStack
import math

import numpy as np
import concourse.bass as bass
from concourse import mybir

F = mybir.dt.float32
R = mybir.dt.float32r
ALU = mybir.AluOpType
ACT = mybir.ActivationFunctionType
AX_X = mybir.AxisListType.X

P = 128
T = 512
TB = T // P
D = 1024
KT = D // P
FF = 2816
HALF = FF // P // 2
EPS = 1e-6
NEG = -1e30
SP_CAP = 30.0

SB_H, SB_D = 8, 64
GLA_H, GLA_DV, GLA_C = 4, 128, 64
ATT_H = 8
ML_H = 8

PAR_COLS = {}
_n = 0
for _name, _w in (("norm_mix", KT), ("b_gate", 16), ("b_alpha", 2), ("gla_g", 4), ("norm_ffn", KT),
                  ("conv_w", 3 * 22), ("conv_b", 22), ("norm_final", KT), ("c", KT), ("ada_b", 96),
                  ("b_pool", 4), ("pool_scale", 4), ("q_gain", 1), ("k_gain", 1), ("od_conv_w", 40),
                  ("od_conv_b", 8), ("gate_b", 2), ("head_gain", 8), ("eps", 1)):
    PAR_COLS[_name] = (_n, _w)
    _n += _w
PAR_W = _n

CST_COLS = {}
_n = 0
for _name, _w in (("ident", P), ("ntri", P), ("ones", P), ("nones", P), ("neg_strict", P), ("keep_strict", P),
                  ("gla_mask", P), ("bd64", P), ("rot", P), ("neg_fwd", P), ("neg_bwd", P)):
    CST_COLS[_name] = (_n, _w)
    _n += _w
CST_W = _n
GLA_W = T + 256
ROPE_W = 2 * T
POOL_W = 5 * T
PAD = 8

WIDTH = {"F": 2048, "T": 2048, "KV": 2048, "S": 1024, "B": 1024, "D": HALF * P}
STAGES = [("sb_q", "F", 2), ("sb_k", "F", 2), ("sb_v", "T", 2),
          ("g_q", "F", 1), ("g_k", "F", 1),
          ("g_v", "T", 2), ("g_r", "F", 2), ("g_a", "S", 1), ("gates", "F", 8), ("branch", "B", 8),
          ("out", "F", 4), ("up0", "F", HALF), ("down0", "D", KT), ("up1", "F", HALF), ("down1", "D", KT),
          ("pool_u", "F", 2), ("att_q", "F", 2), ("att_kv", "KV", 1), ("att_out", "F", 4),
          ("e_up0", "F", HALF), ("e_down0", "D", KT), ("e_up1", "F", HALF), ("e_down1", "D", KT),
          ("ml_qk", "F", 4), ("ml_v", "T", 4), ("ml_g", "S", 1), ("ml_o", "F", 4), ("ml_out", "F", 4),
          ("o_up0", "F", HALF), ("o_down0", "D", KT), ("o_up1", "F", HALF), ("o_down1", "D", KT)]
C0, KIND, COUNT = {}, {}, {}
_c = 0
for _name, _k, _cnt in STAGES:
    C0[_name], KIND[_name], COUNT[_name] = _c, _k, _cnt
    _c += _cnt
N_CHUNKS = _c
ROW0, ROWS = {}, {}
for _name, _k, _cnt in STAGES:
    ROW0[_name] = ROWS.get(WIDTH[_k], 0)
    ROWS[WIDTH[_k]] = ROW0[_name] + _cnt
ADA_N = 24


def end_of(stage):
    return C0[stage] + COUNT[stage]


def build(nc, xT, w2048, w1024, w1408, ada, par_d, cst_d, gla_d, rope_d, pool_d, outT):
    with ExitStack() as ctx:
        def sb(name, shape, dt=F):
            return ctx.enter_context(nc.sbuf_tensor(name, shape, dt))

        def sem(name):
            return ctx.enter_context(nc.semaphore(name))

        h = sb("h", [P, KT, T])
        xh, xl = sb("xh", [P, KT, T], R), sb("xl", [P, KT, T], R)
        raw = sb("raw", [P, 2, 2048])
        wh, wl = sb("wh", [P, 2, 2048], R), sb("wl", [P, 2, 2048], R)
        zh, zl = sb("zh", [P, HALF, T], R), sb("zl", [P, HALF, T], R)
        par, cst = sb("par", [P, PAR_W]), sb("cst", [P, CST_W])
        mod = sb("mod", [P, 2, 48])
        cond = sb("cond", [P, KT])
        small = sb("small", [P, 256])
        arena = sb("arena", [P, 28, T])
        pairs = ctx.enter_context(nc.psum_tensor("pairs", [P, 4, T], F))
        aux = ctx.enter_context(nc.psum_tensor("aux", [P, 4, T], F))

        def pc(name, i=0, n=1):
            return par[:, PAR_COLS[name][0] + i:PAR_COLS[name][0] + i + n]

        def pc_at(name, i):
            return par[:, bass.ds(i + PAR_COLS[name][0], 1)]

        def cm(name):
            return cst[:, CST_COLS[name][0]:CST_COLS[name][0] + CST_COLS[name][1]]

        raw_full = [sem("raw_full0"), sem("raw_full1")]
        hi_done, lo_done = sem("hi_done"), sem("lo_done")
        mm_done = sem("mm_done")
        drained = sem("drained")
        consts = sem("consts")
        x_in = [sem(f"x_in{i}") for i in range(4)]
        stored = sem("stored")

        def chunk_loop(eng, stage, body, lo=0, hi=None):
            c0 = C0[stage]
            c, end = c0 + lo, c0 + (COUNT[stage] if hi is None else hi)
            while c < end and c < 2:
                body(c, c % 2, c - c0)
                c += 1
            pairs_n = (end - c) // 2
            if pairs_n > 1:
                with eng.Fori(0, pairs_n) as i:
                    body(i * 2 + c, c % 2, i * 2 + (c - c0))
                    body(i * 2 + (c + 1), (c + 1) % 2, i * 2 + (c + 1 - c0))
            elif pairs_n == 1:
                body(c, c % 2, c - c0)
                body(c + 1, (c + 1) % 2, c + 1 - c0)
            c += 2 * pairs_n
            if c < end:
                body(c, c % 2, c - c0)

        def is_static(c):
            return isinstance(c, int)

        S = {}

        def s(name):
            if name not in S:
                S[name] = sem(name)
            return S[name]

        NORM_OF = {"n_mix": 0, "n_ffn": 1, "n_final": 2, "n_e1": 3, "n_e2": 4, "n_o1": 5, "n_o2": 6}
        NORM_AFTER = {"n_mix": None, "n_ffn": "out", "n_final": "down1", "n_e1": None, "n_e2": "att_out",
                      "n_o1": "e_down1", "n_o2": "ml_out"}
        SQ_GROUPS = {"n_mix": (4, 2), "n_ffn": (4, 2), "n_final": (8, 1), "n_e1": (8, 1), "n_e2": (4, 2),
                     "n_o1": (8, 1), "n_o2": (4, 2)}
        SQ_BASE, base = {}, 0
        for name, (count, _) in SQ_GROUPS.items():
            SQ_BASE[name] = base
            base += count
        NORM_OF_STAGE = {stage: name for name, stage in NORM_AFTER.items() if stage}
        sq_zero = s("sq_zero")
        sq_done, sq_acc = s("sq_done"), s("sq_acc")
        sq_sum = s("sq_sum")
        rstd_done = s("rstd_done")
        xn_done, xh_done, x_ready = s("xn_done"), s("xh_done"), s("x_ready")
        h_final = s("h_final")
        SQ = [arena[:, 22:24, :], arena[:, 24:26, :]]
        SQ_ACC = arena[:, 26:28, :]
        RSTD = arena[:, 2, :]
        LNV = arena[:, 3, :]
        XN = arena[:, 4:6, :]

        def norm_cols(name):
            if name in ("n_mix", "n_ffn", "n_final"):
                key = {"n_mix": "norm_mix", "n_ffn": "norm_ffn", "n_final": "norm_final"}[name]
                return (lambda k: pc(key, k)), None
            layer, second = (0, 1) if name[2] == "e" else (1, 1)
            base = 0 if name[3] == "1" else 24
            return ((lambda k: mod[:, layer, base + 8 + k:base + 9 + k]),
                    (lambda k: mod[:, layer, base + k:base + k + 1]))

        def square(a, name, g, tiles, slot):
            if not (is_static(g) and g < 2):
                a.wait_ge(sq_acc, g - 1)
            a.wait_ge(consts, 32)
            a.activation(SQ[slot][:, 0:SQ_GROUPS[name][1], :], tiles, ACT.Square).then_inc(sq_done, 1)

        def square_zero(v, name):
            if NORM_OF[name]:
                v.wait_ge(sq_sum, NORM_OF[name])
            v.memset(SQ_ACC, 0.0).then_inc(sq_zero, 1)
            v.wait_ge(sq_zero, NORM_OF[name] + 1)

        def square_add(v, name, g, slot):
            w = SQ_GROUPS[name][1]
            v.wait_ge(sq_done, g + 1)
            if not (is_static(g) and g < 1):
                v.wait_ge(sq_acc, g)
            v.tensor_tensor(SQ_ACC[:, 0:w, :], SQ_ACC[:, 0:w, :], SQ[slot][:, 0:w, :], ALU.add).then_inc(sq_acc, 1)

        def norm_act(a, name):
            n = NORM_OF[name]
            if name == "n_mix":
                a.wait_ge(consts, 32)
                for i in range(4):
                    a.wait_ge(x_in[i], 16)
                    square(a, name, i, h[:, 2 * i:2 * i + 2, :], i % 2)
                hi_part(a, 0, 0)
            elif name == "n_e1":
                for k in range(KT):
                    a.wait_ge(h_final, k + 1)
                    square(a, name, SQ_BASE[name] + k, h[:, k:k + 1, :], k % 2)
            a.preload_act_table_set("natural_log_exp_and_others")
            a.wait_ge(sq_sum, n + 1)
            a.activation(LNV, aux[:, 0, :], ACT.Ln, scale=1.0 / D, bias=pc("eps")).then_inc(s("norm_ln"), 1)
            a.wait_ge(s("norm_ln"), n + 1)
            a.activation(RSTD, LNV, ACT.Exp, scale=-0.5).then_inc(rstd_done, 1)
            if name == "n_final":
                return
            _, shift = norm_cols(name)
            m = n if n < 2 else n - 1
            for k in range(KT):
                a.wait_ge(xn_done, KT * m + k + 1)
                if shift is None:
                    a.activation(xh[:, k, :], XN[:, k % 2, :], ACT.Copy).then_inc(xh_done, 1)
                else:
                    a.activation(xh[:, k, :], XN[:, k % 2, :], ACT.Identity, bias=shift(k)).then_inc(xh_done, 1)

        def norm_pe(p, name):
            n = NORM_OF[name]
            groups, w = SQ_GROUPS[name]
            if n:
                p.wait_ge(rstd_done, n)
            p.wait_ge(consts, 32)
            p.wait_ge(sq_acc, SQ_BASE[name] + groups)
            for i in range(w):
                mm = p.matmul(aux[:, 0, :], cm("ones"), SQ_ACC[:, i, :], start=(i == 0), stop=(i == w - 1))
            mm.then_inc(sq_sum, 1)

        def norm_dve(v, name):
            n = NORM_OF[name]
            scale, shift = norm_cols(name)
            if name == "n_mix":
                square_zero(v, name)
                for i in range(4):
                    square_add(v, name, i, i % 2)
            v.wait_ge(rstd_done, n + 1)
            if name == "n_final":
                square_zero(v, "n_e1")
                for k in range(KT + 1):
                    if k < KT:
                        v.scalar_tensor_tensor(h[:, k, :], h[:, k, :], scale(k), RSTD, ALU.mult, ALU.mult
                                               ).then_inc(h_final, 1)
                    if k:
                        square_add(v, "n_e1", SQ_BASE["n_e1"] + k - 1, (k - 1) % 2)
                return
            m = n if n < 2 else n - 1
            for k in range(KT + 1):
                if k < KT:
                    if k >= 2:
                        v.wait_ge(x_ready, KT * m + k - 1)
                    v.scalar_tensor_tensor(XN[:, k % 2, :], h[:, k, :], scale(k), RSTD, ALU.mult, ALU.mult
                                           ).then_inc(xn_done, 1)
                if k:
                    v.wait_ge(xh_done, KT * m + k)
                    src, dst = XN[:, (k - 1) % 2, :], xl[:, k - 1, :]
                    hi = xh[:, k - 1, :].bitcast(F)
                    if shift is None:
                        v.tensor_tensor(dst, src, hi, ALU.subtract).then_inc(x_ready, 1)
                    else:
                        v.scalar_tensor_tensor(dst, src, shift(k - 1), hi, ALU.add, ALU.subtract
                                               ).then_inc(x_ready, 1)

        def hi_part(a, c, slot):
            a.wait_ge(raw_full[slot], c * 8 + (16 if slot == 0 else 8))
            if not (is_static(c) and c < 2):
                a.wait_ge(mm_done, c - 1)
            a.activation(wh[:, slot, :], raw[:, slot, :], ACT.Copy).then_inc(hi_done, 1)

        def linear_pe(p, stage, ready=None, norm=None):
            kind = KIND[stage]
            if ready:
                p.wait_ge(*ready)
            passes = ((wh, 0), (wl, 0), (wh, 1))

            def first(c, slot, l):
                p.wait_ge(lo_done, c + 1)
                if not (is_static(c) and c < 2):
                    p.wait_ge(drained, c - 1)
                for k in range(KT):
                    p.wait_ge(x_ready, KT * norm + k + 1)
                    for m in range(2):
                        for w, part in passes:
                            at = k * 256 + m * P
                            mm = p.matmul(pairs[:, 2 * slot + m, :], w[:, slot, at:at + P], (xh, xl)[part][:, k, :],
                                          start=(k == 0 and w is wh and part == 0), stop=(k == KT - 1 and part == 1))
                mm.then_inc(mm_done, 1)
                ada_step_pe(c, slot, l)

            def ada_step_pe(c, slot, l):
                if stage in ADA_OF:
                    ada_pe(p, l + (ADA_OF[stage] - 1), 1 - ada_slot(stage, slot), 0 if ADA_OF[stage] < ADA_N else 1)

            def body(c, slot, l):
                p.wait_ge(lo_done, c + 1)
                if not (is_static(c) and c < 2):
                    p.wait_ge(drained, c - 1)
                src = (zh, zl) if stage in ("att_out", "ml_out") else (xh, xl)
                if kind in ("F", "KV"):
                    for m in range(2 if kind == "F" else 1):
                        for k in range(KT):
                            for w, part in passes:
                                at = k * 256 + m * P
                                mm = p.matmul(pairs[:, 2 * slot + m, :], w[:, slot, at:at + P], src[part][:, k, :],
                                              start=(k == 0 and w is wh and part == 0),
                                              stop=(k == KT - 1 and part == 1))
                if kind in ("T", "KV"):
                    n = 256 if kind == "T" else P
                    for tb in range(TB):
                        if kind == "T":
                            dst = pairs[:, 2 * slot + tb // 2, (tb % 2) * 256:(tb % 2) * 256 + 256]
                        else:
                            dst = pairs[:, 2 * slot + 1, tb * P:(tb + 1) * P]
                        for k in range(KT):
                            for w, part in passes:
                                at = k * 256 + (0 if kind == "T" else P)
                                mm = p.matmul(dst, src[part][:, k, tb * P:(tb + 1) * P], w[:, slot, at:at + n],
                                              start=(k == 0 and w is wh and part == 0),
                                              stop=(k == KT - 1 and part == 1))
                if kind in ("S", "B", "D"):
                    src = (xh, xl) if kind == "S" else (zh, zl)
                    tiles = {"S": [range(KT)], "B": [range(4), range(4, 8)], "D": [range(HALF)]}[kind]
                    for m, ks in enumerate(tiles):
                        for k in ks:
                            for w, part in passes:
                                mm = p.matmul(pairs[:, 2 * slot + m, :], w[:, slot, k * P:(k + 1) * P],
                                              src[part][:, k, :],
                                              start=(k == ks[0] and w is wh and part == 0),
                                              stop=(k == ks[-1] and part == 1))
                mm.then_inc(mm_done, 1)
                ada_step_pe(c, slot, l)
            if norm is None:
                chunk_loop(p, stage, body)
            else:
                chunk_loop(p, stage, first, hi=1)
                chunk_loop(p, stage, body, lo=1)

        def hi_only(a, stage):
            last = 1 if end_of(stage) == N_CHUNKS else 0
            norm = NORM_OF_STAGE.get(stage)

            def body(c, slot, l):
                hi_part(a, c + 1, 1 - slot)
                if norm:
                    w = SQ_GROUPS[norm][1]
                    a.wait_ge(drained, c + 1)
                    square(a, norm, l + SQ_BASE[norm], h[:, bass.ds(l * w, w), :], slot)
            chunk_loop(a, stage, body, hi=COUNT[stage] - last)

        def drain_copy(v, stage, dst, scale=1.0):
            def body(c, slot, l):
                v.wait_ge(mm_done, c + 1)
                src = pairs[:, 2 * slot:2 * slot + 2, :]
                if KIND[stage] == "T":
                    src = src.rearrange("p b (t n) -> p (b t) n", n=256)
                v.tensor_scalar(dst(l), src, scale, None, ALU.mult).then_inc(drained, 1)
            chunk_loop(v, stage, body)

        def drain_residual(v, stage, gate=None):
            def body(c, slot, l):
                v.wait_ge(mm_done, c + 1)
                if KIND[stage] == "D":
                    tile = h[:, bass.ds(l, 1), :]
                    if gate is None:
                        v.tensor_tensor(tile, pairs[:, 2 * slot:2 * slot + 1, :], tile, ALU.add).then_inc(drained, 1)
                    else:
                        v.scalar_tensor_tensor(tile, pairs[:, 2 * slot:2 * slot + 1, :], gate(l), tile,
                                               ALU.mult, ALU.add).then_inc(drained, 1)
                elif gate is None:
                    tile = h[:, bass.ds(l * 2, 2), :]
                    v.tensor_tensor(tile, pairs[:, 2 * slot:2 * slot + 2, :], tile, ALU.add).then_inc(drained, 1)
                else:
                    for m in range(2):
                        tile = h[:, bass.ds(l * 2 + m, 1), :]
                        ins = v.scalar_tensor_tensor(tile, pairs[:, 2 * slot + m:2 * slot + m + 1, :],
                                                     gate(l * 2 + m), tile, ALU.mult, ALU.add)
                    ins.then_inc(drained, 1)
            norm = NORM_OF_STAGE.get(stage)

            def body_add(c, slot, l):
                body(c, slot, l)
                square_add(v, norm, l + (SQ_BASE[norm] - 1), 1 - slot)
            if norm:
                square_zero(v, norm)
                chunk_loop(v, stage, body, hi=1)
                chunk_loop(v, stage, body_add, lo=1)
                last = COUNT[stage] - 1
                square_add(v, norm, SQ_BASE[norm] + last, (C0[stage] + last) % 2)
            else:
                chunk_loop(v, stage, body)

        UP_N = {"up0": 0, "up1": 1, "e_up0": 2, "e_up1": 3, "o_up0": 4, "o_up1": 5}
        a_copied, conv_done, act_done = s("a_copied"), s("conv_done"), s("act_done")
        hid_done, hid_hi, conv_step = s("hid_done"), s("hid_hi"), s("conv_step")
        APAD = arena[:, 0:4, :].rearrange("p a b -> p (a b)")
        apad = [APAD[:, i * 1024:i * 1024 + T + 2] for i in range(2)]
        CONV = arena[:, 4:6, :]
        ACTV = arena[:, 6:8, :]
        HID = arena[:, 8:10, :]

        def up_act(a, stage):
            first = stage in ("up0", "up1")
            n0 = UP_N[stage] * HALF

            def last(c, slot, l):
                body(c, slot, l, ahead=False)

            def body(c, slot, l, ahead=True):
                a.wait_ge(mm_done, c + 1)
                f = l + n0
                if first:
                    a.activation(apad[slot][:, 2:T + 2], pairs[:, 2 * slot, :], ACT.Copy).then_inc(a_copied, 1)
                    if ahead:
                        hi_part(a, c + 2, slot)
                    a.wait_ge(conv_done, f + 1)
                    a.activation(ACTV[:, slot, :], CONV[:, slot, :], ACT.Gelu_apprx_tanh).then_inc(act_done, 1)
                else:
                    a.activation(ACTV[:, slot, :], pairs[:, 2 * slot, :], ACT.Silu).then_inc(act_done, 1)
                    if ahead:
                        hi_part(a, c + 2, slot)
                a.wait_ge(hid_done, f + 1)
                a.wait_ge(consts, 32)
                a.activation(zh[:, bass.ds(l, 1), :], HID[:, slot:slot + 1, :], ACT.Copy).then_inc(hid_hi, 1)
            hi_part(a, C0[stage] + 1, (C0[stage] + 1) % 2)
            chunk_loop(a, stage, body, hi=COUNT[stage] - 1)
            chunk_loop(a, stage, last, lo=COUNT[stage] - 1)

        def up_dve(v, stage):
            first = stage in ("up0", "up1")
            n0 = UP_N[stage] * HALF
            half = HALF if stage in ("up1",) else 0

            def body(c, slot, l):
                f = l + n0
                if stage in ADA_OF:
                    ada_dve(v, l + ADA_OF[stage], ada_slot(stage, slot))
                if first:
                    v.wait_ge(a_copied, f + 1)
                    w = lambda tap: pc_at("conv_w", l + (tap * 22 + half))
                    v.tensor_scalar(CONV[:, slot, :], apad[slot][:, 0:T], w(0), pc_at("conv_b", l + half),
                                    ALU.mult, ALU.add).then_inc(conv_step, 1)
                    v.wait_ge(conv_step, f * 2 + 1)
                    v.scalar_tensor_tensor(CONV[:, slot, :], apad[slot][:, 1:T + 1], w(1), CONV[:, slot, :],
                                           ALU.mult, ALU.add).then_inc(conv_step, 1)
                    v.wait_ge(conv_step, f * 2 + 2)
                    v.scalar_tensor_tensor(CONV[:, slot, :], apad[slot][:, 2:T + 2], w(2), CONV[:, slot, :],
                                           ALU.mult, ALU.add).then_inc(conv_done, 1)
                v.wait_ge(act_done, f + 1)
                v.tensor_tensor(HID[:, slot, :], ACTV[:, slot, :], pairs[:, 2 * slot + 1, :], ALU.mult
                                ).then_inc(hid_done, 1)
                v.wait_ge(hid_hi, f + 1)
                v.tensor_tensor(zl[:, bass.ds(l, 1), :], HID[:, slot:slot + 1, :],
                                zh[:, bass.ds(l, 1), :].bitcast(F), ALU.subtract).then_inc(drained, 1)
            chunk_loop(v, stage, body)

        ada_full = [sem("ada_full0"), sem("ada_full1")]
        ada_step, ada_acc_done, ada_sum = sem("ada_step"), sem("ada_acc_done"), sem("ada_sum")
        ada_raw = arena[:, 10:18, :].rearrange("p (s x) b -> p s (x b)", s=2)
        ada_acc = sb("ada_acc", [P, 2, 256])
        ADA_OF = {"up0": 2, "up1": 2 + HALF, "e_up0": ADA_N + 2, "e_up1": ADA_N + 2 + HALF}

        def ada_load(sp, A, slot):
            if not (is_static(A) and A < 2):
                sp.wait_ge(ada_acc_done, A - 1)
            sp.dma_start(ada_raw[:, slot, :], ada[bass.ds(A, 1), :, :].rearrange("a p n -> p (a n)")
                         ).then_inc(ada_full[slot], 16)

        def ada_dve(v, A, slot):
            v.wait_ge(ada_full[slot], A * 8 + (16 if slot == 0 else 8))
            if not (is_static(A) and A < 2):
                v.wait_ge(ada_sum, A - 1)
            acc = ada_acc[:, slot, :]
            v.tensor_scalar(acc, ada_raw[:, slot, 0:256], cond[:, 0:1], None, ALU.mult).then_inc(ada_step, 1)
            for k in range(1, KT):
                v.wait_ge(ada_step, A * (KT - 1) + k)
                v.scalar_tensor_tensor(acc, ada_raw[:, slot, k * 256:(k + 1) * 256], cond[:, k:k + 1], acc,
                                       ALU.mult, ALU.add).then_inc(ada_step if k < KT - 1 else ada_acc_done, 1)

        def ada_pe(p, A, slot, layer):
            p.wait_ge(ada_acc_done, A + 1)
            for m in range(2):
                mm = p.matmul(aux[:, 1, bass.ds((A - layer * ADA_N) * 2 + m, 1)], ada_acc[:, slot, m * P:(m + 1) * P],
                              cm("ones")[:, 0:1], start=True, stop=True)
            mm.then_inc(ada_sum, 1)

        def ada_slot(stage, slot):
            return (slot + C0[stage] + ADA_OF[stage]) % 2

        mod_done = sem("mod_done")

        def mod_dve(v, layer):
            v.wait_ge(ada_sum, ADA_N * (layer + 1))
            v.tensor_tensor(mod[:, layer, :], aux[:, 1, 0:48], pc("ada_b", 48 * layer, 48), ALU.add
                            ).then_inc(mod_done, 1)
            v.wait_ge(mod_done, 2 * layer + 1)
            two = mod[:, layer, :].rearrange("p (a b) -> p a b", a=2)[:, :, 8:16]
            v.tensor_scalar(two, two, 1.0, None, ALU.add).then_inc(mod_done, 1)

        SBQ, SBK = arena[:, 0:4, :], arena[:, 4:8, :]
        SBV = arena[:, 8:12, :]
        SB_EL = arena[:, 12:14, :]
        SB_W = arena[:, 14:16, :]
        SB_SPA = arena[:, 16:19, :].rearrange("p a b -> p (a b)")
        sp_at = [0, 512, 896, 1152]
        SB_SP = [SB_SPA[:, sp_at[i]:sp_at[i] + T - P * i] for i in range(TB)]
        b_qk, b_cap, b_exp, b_ln = sem("b_qk"), sem("b_cap"), sem("b_exp"), sem("b_ln")
        b_max, b_sp, b_tri, b_w, b_pv = sem("b_max"), sem("b_sp"), sem("b_tri"), sem("b_w"), sem("b_pv")
        z_hi, z_lo = sem("z_hi"), sem("z_lo")

        SB_N = SB_H * TB

        def sb_pe(p):
            p.wait_ge(drained, end_of("sb_v"))

            def qk(n):
                hd, i = n // TB, TB - 1 - n % TB
                r = (hd % 2) * SB_D
                if n >= 3:
                    p.wait_ge(b_w, n - 2)
                p.matmul(aux[:, n % 3, 0:T - P * i], SBK[r:r + SB_D, hd // 2, i * P:(i + 1) * P],
                         SBQ[r:r + SB_D, hd // 2, i * P:T], start=True, stop=True).then_inc(b_qk, 1)

            def tri(n):
                hd, i = n // TB, TB - 1 - n % TB
                w = T - P * i
                p.wait_ge(b_sp, n + 1)
                p.matmul(aux[:, n % 3, 0:w], cm("ntri"), SB_SP[i], start=False, stop=False,
                         skip_group_check=True)
                for j in range(i + 1, TB):
                    p.matmul(aux[:, n % 3, (j - i) * P:w], cm("nones"), SB_SP[j], start=False, stop=False,
                             skip_group_check=True)
                p.matmul(aux[:, n % 3, 0:P], cm("ident"), cm("neg_strict"), start=False, stop=True,
                         skip_group_check=True).then_inc(b_tri, 1)

            def pv(n):
                hd, i = n // TB, TB - 1 - n % TB
                r = (hd % 2) * SB_D
                p.wait_ge(b_w, n + 1)
                if n % (2 * TB) == 0 and n:
                    p.wait_ge(z_lo, n // (2 * TB))
                p.matmul(aux[r:r + SB_D, 3, i * P:T], SBV[:, i, hd * SB_D:(hd + 1) * SB_D], SB_W[:, n % 2, 0:T - P * i],
                         start=(i == TB - 1), stop=(i == 0), skip_group_check=True).then_inc(b_pv, 1)

            qk(0)
            qk(1)
            for n in range(SB_N):
                tri(n)
                if n:
                    pv(n - 1)
                if n + 2 < SB_N:
                    qk(n + 2)
            pv(SB_N - 1)

        def sb_act(a):
            a.preload_act_table_set("natural_log_exp_and_others")

            def weights(n):
                w = T - P * (TB - 1 - n % TB)
                a.wait_ge(b_tri, n + 1)
                if n >= 2:
                    a.wait_ge(b_pv, n - 1)
                a.activation(SB_W[:, n % 2, 0:w], aux[:, n % 3, 0:w], ACT.Exp).then_inc(b_w, 1)

            def out_hi(pr):
                a.wait_ge(b_pv, 2 * TB * (pr + 1))
                a.activation(zh[:, pr, :], aux[:, 3, :], ACT.Copy).then_inc(z_hi, 1)

            for n in range(SB_N):
                w = T - P * (TB - 1 - n % TB)
                el = SB_EL[:, n % 2, 0:w]
                a.wait_ge(b_cap, n + 1)
                a.activation(el, el, ACT.Exp).then_inc(b_exp, 1)
                a.wait_ge(b_exp, n + 1)
                a.activation(el, el, ACT.Ln, bias=1.0).then_inc(b_ln, 1)
                if n:
                    weights(n - 1)
                if n % (2 * TB) == 1 and n > 1:
                    out_hi(n // (2 * TB) - 1)
            weights(SB_N - 1)
            out_hi(SB_H // 2 - 1)

        def sb_dve(v):
            def out_lo(pr):
                v.wait_ge(z_hi, pr + 1)
                v.tensor_tensor(zl[:, pr, :], aux[:, 3, :], zh[:, pr, :].bitcast(F), ALU.subtract).then_inc(z_lo, 1)

            for n in range(SB_N):
                i = TB - 1 - n % TB
                w = T - P * i
                el = SB_EL[:, n % 2, 0:w]
                v.wait_ge(b_qk, n + 1)
                v.tensor_scalar(el, aux[:, n % 3, 0:w], SP_CAP, None, ALU.min).then_inc(b_cap, 1)
                v.wait_ge(b_ln, n + 1)
                if n % TB == 0 and n:
                    v.wait_ge(b_tri, n)
                elif n:
                    if n >= TB:
                        v.wait_ge(b_tri, n - n % TB)
                v.tensor_tensor(SB_SP[i], aux[:, n % 3, 0:w], el, ALU.max).then_inc(b_max, 1)
                v.wait_ge(b_max, n + 1)
                v.tensor_tensor(SB_SP[i][:, 0:P], SB_SP[i][:, 0:P], cm("keep_strict"), ALU.mult).then_inc(b_sp, 1)
                if n % (2 * TB) == 1 and n > 1:
                    out_lo(n // (2 * TB) - 1)
            out_lo(SB_H // 2 - 1)

        GQ, GK = arena[:, 0:2, :], arena[:, 2:4, :]
        GV = arena[:, 4:8, :]
        GR = arena[:, 8:12, :]
        G_NX, G_EL, G_CUM = arena[:, 12:14, :], arena[:, 14:16, :], arena[:, 16:18, :]
        G_EQ, G_EK, G_EE = arena[:, 18:20, :], arena[:, 20:22, :], arena[:, 22:24, :]
        G_A = arena[:, 24, :]
        G_CST = arena[:, 25:27, :].rearrange("p a b -> p (a b)")
        G_RESET, G_WA = G_CST[:, 0:T], G_CST[:, T:T + 256]
        G_KT = G_NX
        G_S = arena[:, 24:28, :].rearrange("p (j x) (n v) -> p j (x n) v", j=2, v=P)
        G_AT = [arena[:, 14, :], arena[:, 15, :], arena[:, 20, :], arena[:, 21, :]]
        G_SQ, G_RS, G_T = G_CUM, G_NX, G_EE
        gla_in = sem("gla_in")
        g_pre, g_nx, g_cap, g_e, g_l = sem("g_pre"), sem("g_nx"), sem("g_cap"), sem("g_e"), sem("g_l")
        g_sp, g_cum, g_eqk, g_diff, g_ee = sem("g_sp"), sem("g_cum"), sem("g_eqk"), sem("g_diff"), sem("g_ee")
        g_qd, g_ki, g_ke, g_tr, g_kt = sem("g_qd"), sem("g_ki"), sem("g_ke"), sem("g_tr"), sem("g_kt")
        g_att, g_at, g_ds, g_st, g_o = sem("g_att"), sem("g_at"), sem("g_ds"), sem("g_st"), sem("g_o")
        g_sq, g_ms, g_ln, g_rs, g_t1 = sem("g_sq"), sem("g_ms"), sem("g_ln"), sem("g_rs"), sem("g_t1")
        g_t2, g_silu = sem("g_t2"), sem("g_silu")
        GN = T // GLA_C
        STEPS = [(j, c) for j in range(2) for c in range(GN - 1)]
        g_in = sem("g_in")

        def gla_pe(p):
            p.wait_ge(drained, end_of("g_a"))
            p.wait_ge(gla_in, 16)
            for j in range(2):
                p.matmul(aux[:, j, :], G_WA[0:16, j * P:(j + 1) * P], G_A[0:16, :], start=True, stop=True
                         ).then_inc(g_pre, 1)
            for j in range(2):
                p.wait_ge(g_ke, 1)
                for tb in range(TB):
                    mm = p.transpose(aux[:, 2 + j, tb * P:(tb + 1) * P], G_EE[:, j, tb * P:(tb + 1) * P], cm("ident"))
                mm.then_inc(g_tr, 1)
            p.wait_ge(g_ki, 1)
            for hd in range(GLA_H):
                r, j = (hd % 2) * 64, hd // 2
                if hd >= 2:
                    p.wait_ge(g_at, hd - 1)
                for tb in range(TB):
                    c = slice(tb * P, (tb + 1) * P)
                    mm = p.matmul(aux[:, hd % 2, c], GK[r:r + 64, j, c], GQ[r:r + 64, j, c], start=True, stop=True)
                mm.then_inc(g_att, 1)
            p.wait_ge(g_kt, 2)
            for n, (j, c) in enumerate(STEPS):
                r, k = (c % 2) * 64, c // 2
                if n >= 2:
                    p.wait_ge(g_st, n - 1 if c else n)
                p.matmul(aux[:, 2 + c % 2, 0:256], G_KT[r:r + 64, j, k * P:(k + 1) * P],
                         GV[r:r + 64, k, j * 256:(j + 1) * 256], start=True, stop=True).then_inc(g_ds, 1)
            p.wait_ge(g_st, 2 * (GN - 1))
            for hd in range(GLA_H + 1):
                if hd < GLA_H:
                    r, j = (hd % 2) * 64, hd // 2
                    p.wait_ge(g_at, GLA_H)
                    if hd >= 2:
                        p.wait_ge(g_t1, hd - 1)
                    for tb in range(TB):
                        c = slice(tb * P, (tb + 1) * P)
                        mm = p.matmul(aux[:, hd % 2, c], GV[:, tb, hd * P:(hd + 1) * P], G_AT[hd][:, c],
                                      start=(tb == 0), stop=True, skip_group_check=True)
                    mm.then_inc(g_in, 1)
                    p.wait_ge(g_in, hd + 1)
                    for n in range(1, GN):
                        mm = p.matmul(aux[:, hd % 2, n * 64:(n + 1) * 64], G_S[r:r + 64, j, n, :],
                                      GQ[r:r + 64, j, n * 64:(n + 1) * 64], start=False, stop=True,
                                      skip_group_check=True)
                    mm.then_inc(g_o, 1)
                if hd:
                    q = hd - 1
                    p.wait_ge(g_sq, q + 1)
                    if q >= 2:
                        p.wait_ge(g_ln, q - 1)
                    p.matmul(aux[:, 2 + q % 2, :], cm("ones"), G_SQ[:, q % 2, :], start=True, stop=True
                             ).then_inc(g_ms, 1)

        def gla_act(a):
            a.wait_ge(drained, end_of("g_r"))
            a.activation(GR, GR, ACT.Silu).then_inc(g_silu, 1)
            a.preload_act_table_set("natural_log_exp_and_others")
            a.wait_ge(g_cap, 1)
            a.activation(G_EL, G_EL, ACT.Exp).then_inc(g_e, 1)
            a.wait_ge(g_e, 1)
            a.activation(G_EL, G_EL, ACT.Ln, bias=1.0).then_inc(g_l, 1)
            a.wait_ge(g_cum, 2)
            a.activation(G_EQ, G_CUM, ACT.Exp, scale=-1.0 / 16).then_inc(g_eqk, 1)
            a.activation(G_EK, G_CUM, ACT.Exp, scale=1.0 / 16).then_inc(g_eqk, 1)
            a.wait_ge(g_diff, 1)
            a.activation(G_EE, G_EE, ACT.Exp, scale=-1.0 / 16).then_inc(g_ee, 1)
            for hd in range(GLA_H + 1):
                if hd < GLA_H:
                    a.wait_ge(g_o, hd + 1)
                    if hd >= 2:
                        a.wait_ge(g_ms, hd - 1)
                    a.activation(G_SQ[:, hd % 2, :], aux[:, hd % 2, :], ACT.Square).then_inc(g_sq, 1)
                if hd:
                    q = hd - 1
                    a.wait_ge(g_ms, q + 1)
                    if q >= 2:
                        a.wait_ge(g_t1, q - 1)
                    rs = G_RS[:, q % 2, :]
                    a.activation(rs, aux[:, 2 + q % 2, :], ACT.Ln, scale=1.0 / GLA_DV, bias=pc("eps")).then_inc(g_ln, 1)
                    a.wait_ge(g_ln, q + 1)
                    a.activation(rs, rs, ACT.Exp, scale=-0.5).then_inc(g_rs, 1)
                    a.wait_ge(g_t2, q + 1)
                    a.activation(zh[:, 4 + q, :], G_T[:, q % 2, :], ACT.Copy).then_inc(z_hi, 1)

        def gla_dve(v):
            v.wait_ge(g_pre, 2)
            v.wait_ge(gla_in, 16)
            for j in range(2):
                v.tensor_scalar(G_NX[:, j, :], aux[:, j, :], -1.0, pc("b_alpha", j), ALU.mult, ALU.subtract
                                ).then_inc(g_nx, 1)
            v.wait_ge(g_nx, 2)
            v.tensor_scalar(G_EL, G_NX, SP_CAP, None, ALU.min).then_inc(g_cap, 1)
            v.wait_ge(g_l, 1)
            v.tensor_tensor(G_NX, G_NX, G_EL, ALU.max).then_inc(g_sp, 1)
            v.wait_ge(g_sp, 1)
            for j in range(2):
                v.tensor_tensor_scan(G_CUM[:, j, :], G_RESET, G_NX[:, j, :], 0.0, ALU.mult, ALU.add
                                     ).then_inc(g_cum, 1)
            v.wait_ge(g_cum, 2)
            cum = G_CUM.rearrange("p j (n c) -> p (j n) c", c=GLA_C)
            v.tensor_tensor(G_EE.rearrange("p j (n c) -> p (j n) c", c=GLA_C),
                            cum[:, :, GLA_C - 1:GLA_C].to_broadcast([P, 2 * GN, GLA_C]), cum, ALU.subtract
                            ).then_inc(g_diff, 1)
            v.wait_ge(g_ee, 1)
            v.tensor_tensor(G_EE, GK, G_EE, ALU.mult).then_inc(g_ke, 1)
            v.wait_ge(g_eqk, 2)
            v.tensor_tensor(GQ, GQ, G_EQ, ALU.mult)
            v.wait_ge(g_ke, 1)
            v.tensor_tensor(GK, GK, G_EK, ALU.mult).then_inc(g_ki, 1)
            v.wait_ge(g_tr, 2)
            v.tensor_copy(G_KT, aux[:, 2:4, :]).then_inc(g_kt, 2)
            v.wait_ge(g_ki, 1)
            for hd in range(GLA_H):
                v.wait_ge(g_att, hd + 1)
                v.tensor_tensor(G_AT[hd].rearrange("p (b c) -> p b c", c=P),
                                aux[:, hd % 2, :].rearrange("p (b c) -> p b c", c=P),
                                cm("gla_mask").rearrange("p (a c) -> p a c", a=1).to_broadcast([P, TB, P]), ALU.mult
                                ).then_inc(g_at, 1)
            for n, (j, c) in enumerate(STEPS):
                v.wait_ge(g_ds, n + 1)
                if c:
                    v.wait_ge(g_st, n)
                for r in (0, 64):
                    inc = aux[r:r + 64, 2 + c % 2, 2 * r:2 * r + P]
                    new = G_S[r:r + 64, j, c + 1, :]
                    if c == 0:
                        ins = v.tensor_copy(new, inc)
                    else:
                        end = c * GLA_C + GLA_C - 1
                        ins = v.scalar_tensor_tensor(new, G_S[r:r + 64, j, c, :], G_EQ[r:r + 64, j, end:end + 1],
                                                     inc, ALU.mult, ALU.add)
                ins.then_inc(g_st, 1)
            v.wait_ge(g_silu, 1)
            for hd in range(GLA_H):
                v.wait_ge(g_rs, hd + 1)
                if hd >= 2:
                    v.wait_ge(z_lo, 4 + hd - 1)
                t = G_T[:, hd % 2, :]
                v.scalar_tensor_tensor(t, aux[:, hd % 2, :], pc("gla_g", hd), G_RS[:, hd % 2, :], ALU.mult, ALU.mult
                                       ).then_inc(g_t1, 1)
                v.wait_ge(g_t1, hd + 1)
                v.tensor_tensor(t, t, GR[:, hd, :], ALU.mult).then_inc(g_t2, 1)
                v.wait_ge(z_hi, 4 + hd + 1)
                v.tensor_tensor(zl[:, 4 + hd, :], t, zh[:, 4 + hd, :].bitcast(F), ALU.subtract).then_inc(z_lo, 1)

        GATE = arena[:, 0:16, :]
        BT = arena[:, 16:20, :]
        BY = arena[:, 20:22, :]
        gate_pre, gate_done = sem("gate_pre"), sem("gate_done")
        br_t, br_y, br_hi = sem("br_t"), sem("br_y"), sem("br_hi")

        def gates_dve(v):
            def body(c, slot, l):
                v.wait_ge(mm_done, c + 1)
                for m in range(2):
                    ins = v.tensor_scalar(GATE[:, bass.ds(l * 2 + m, 1), :], pairs[:, 2 * slot + m:2 * slot + m + 1, :],
                                          pc_at("b_gate", l * 2 + m), None, ALU.add)
                ins.then_inc(drained, 1)
            chunk_loop(v, "gates", body)

        def gates_act(a):
            def body(c, slot, l):
                hi_part(a, c + 1, 1 - slot)
                a.wait_ge(drained, c + 1)
                a.wait_ge(consts, 32)
                tile = GATE[:, bass.ds(l * 2, 2), :]
                a.activation(tile, tile, ACT.Sigmoid).then_inc(gate_done, 1)
            chunk_loop(a, "gates", body)

        def branch_dve(v):
            v.wait_ge(gate_done, COUNT["gates"])

            def body(c, slot, l):
                v.wait_ge(mm_done, c + 1)
                for b in range(2):
                    v.tensor_tensor(BT[:, 2 * slot + b:2 * slot + b + 1, :], GATE[:, bass.ds(l + 8 * b, 1), :],
                                    pairs[:, 2 * slot + b:2 * slot + b + 1, :], ALU.mult).then_inc(br_t, 1)
                v.wait_ge(br_t, l * 2 + 2)
                v.tensor_tensor(BY[:, slot, :], BT[:, 2 * slot, :], BT[:, 2 * slot + 1, :], ALU.add).then_inc(br_y, 1)
                v.wait_ge(br_hi, l + 1)
                v.tensor_tensor(xl[:, bass.ds(l, 1), :], BY[:, slot:slot + 1, :], xh[:, bass.ds(l, 1), :].bitcast(F),
                                ALU.subtract).then_inc(drained, 1)
            chunk_loop(v, "branch", body)

        def branch_act(a):
            def body(c, slot, l):
                hi_part(a, c + 1, 1 - slot)
                a.wait_ge(br_y, l + 1)
                a.wait_ge(consts, 32)
                a.activation(xh[:, bass.ds(l, 1), :], BY[:, slot:slot + 1, :], ACT.Copy).then_inc(br_hi, 1)
            chunk_loop(a, "branch", body)

        UW = T + 2 * PAD
        UP = arena[:, 0:5, :].rearrange("p a b -> p (a b)")[:, 0:4 * UW].rearrange("p (g u) -> p g u", u=UW)
        AQ = arena[:, 5:9, :]
        AKD = arena[:, 9:11, :]
        AV = arena[:, 11, :].rearrange("p (b n) -> p b n", n=P)
        ROPE = arena[:, 12:14, :]
        WPOOL = arena[:, 14, :]
        AP_ = arena[:, 15:17, :]
        APT = arena[:, 17:21, :]
        AK = arena[:, 21, :]
        A_SQ, A_RS, A_QN = arena[:, 22, :], arena[:, 23, :], arena[:, 24, :]
        A_T1, A_T2 = arena[:, 25, :], arena[:, 26, :]
        POOLC = arena[:, 17:22, :]
        PW = [arena[:, 22:24, :].rearrange("p a b -> p (a b)"), arena[:, 24:26, :].rearrange("p a b -> p (a b)")]
        pool_in, rope_in = sem("pool_in"), sem("rope_in")
        u_zero, u_step, u_pooled, u_mm, u_out = (sem("u_zero"), sem("u_step"), sem("u_pooled"), sem("u_mm"),
                                                 sem("u_out"))

        def pool_dve(v):
            v.wait_ge(pool_in, 16)
            done = 0
            v.tensor_copy(WPOOL, POOLC[:, 4, :]).then_inc(u_step, 1)
            done += 1
            for g in range(4):
                src = UP[:, g, :]
                size = UW
                if g:
                    v.wait_ge(u_pooled, g)
                for lev in range(g + 1):
                    step = 1 << lev
                    size -= step
                    dst = PW[lev % 2][:, 0:size]
                    v.wait_ge(u_step, done)
                    v.tensor_tensor(dst, src[:, 0:size], src[:, step:step + size], ALU.add).then_inc(u_step, 1)
                    done += 1
                    src = dst
                at = PAD - (1 << g)
                v.wait_ge(u_step, done)
                v.tensor_tensor(PW[(g + 1) % 2][:, 0:T], src[:, at:at + T], POOLC[:, g, :], ALU.mult
                                ).then_inc(u_step, 1)
                done += 1
                v.wait_ge(u_step, done)
                own = UP[:, g, PAD:PAD + T]
                v.tensor_tensor(own, PW[(g + 1) % 2][:, 0:T], own, ALU.subtract).then_inc(u_pooled, 1)

        def pool_pe(p):
            p.wait_ge(u_pooled, 4)
            for g in range(4):
                p.matmul(aux[:, g, :], WPOOL[:, g * P:(g + 1) * P], UP[:, g, PAD:PAD + T], start=True, stop=True
                         ).then_inc(u_mm, 1)

        def pool_out_dve(v):
            for g in range(5):
                if g < 4:
                    v.wait_ge(u_mm, g + 1)
                    v.tensor_scalar(UP[:, g, PAD:PAD + T], aux[:, g, :], pc("b_pool", g), pc("pool_scale", g),
                                    ALU.add, ALU.mult).then_inc(u_out, 1)
                if g:
                    v.wait_ge(z_hi, 8 + g)
                    v.tensor_tensor(zl[:, g - 1, :], UP[:, g - 1, PAD:PAD + T], zh[:, g - 1, :].bitcast(F),
                                    ALU.subtract).then_inc(z_lo, 1)

        def pool_out_act(a):
            for g in range(4):
                a.wait_ge(u_out, g + 1)
                a.activation(zh[:, g, :], UP[:, g, PAD:PAD + T], ACT.Copy).then_inc(z_hi, 1)

        r_sq, r_ms, r_ln, r_rs, r_qn = sem("r_sq"), sem("r_ms"), sem("r_ln"), sem("r_rs"), sem("r_qn")
        r_rot, r_t1, r_t2, r_out = sem("r_rot"), sem("r_t1"), sem("r_t2"), sem("r_out")
        e_z, e_max, e_p, e_rc, e_pn = sem("e_z"), sem("e_max"), sem("e_p"), sem("e_rc"), sem("e_pn")
        e_t, e_tc, e_pv = sem("e_t"), sem("e_tc"), sem("e_pv")
        A_MAX, A_SUM, A_RC = small[:, 0:32], small[:, 32:64], small[:, 64:96]
        AN = ATT_H * TB

        def rope_src(x):
            return AQ[:, x, :] if x < 4 else AK

        def att_pe(p):
            p.wait_ge(u_out, 4)
            for x in range(5):
                p.wait_ge(r_sq, x + 1)
                if x:
                    p.wait_ge(r_ln, x)
                p.matmul(aux[:, 0, :], cm("bd64"), A_SQ, start=True, stop=True).then_inc(r_ms, 1)
                p.wait_ge(r_qn, x + 1)
                if x:
                    p.wait_ge(r_t2, x)
                p.matmul(aux[:, 1, :], cm("rot"), A_QN, start=True, stop=True).then_inc(r_rot, 1)
            p.wait_ge(r_out, 5)

            def scores(n):
                hd, tb = n // TB, n % TB
                r = (hd % 2) * 64
                if n >= 2:
                    p.wait_ge(e_p, n - 1)
                p.matmul(aux[:, n % 2, :], AQ[r:r + 64, hd // 2, tb * P:(tb + 1) * P],
                         AKD[r:r + 64, hd // 4, :], start=True, stop=True).then_inc(e_z, 1)

            def turn(n):
                p.wait_ge(e_pn, n + 1)
                if n:
                    p.wait_ge(e_tc, n)
                for sb_ in range(TB):
                    mm = p.transpose(aux[:, 2, sb_ * P:(sb_ + 1) * P], AP_[:, n % 2, sb_ * P:(sb_ + 1) * P],
                                     cm("ident"))
                mm.then_inc(e_t, 1)

            def values(hd):
                r = (hd % 2) * 64
                p.wait_ge(e_tc, TB * (hd + 1))
                if hd % 2 == 0 and hd:
                    p.wait_ge(z_lo, 12 + hd // 2)
                for sb_ in range(TB):
                    mm = p.matmul(aux[r:r + 64, 3, :], AV[:, sb_, (hd // 4) * 64:(hd // 4) * 64 + 64], APT[:, sb_, :],
                                  start=(sb_ == 0), stop=(sb_ == TB - 1))
                mm.then_inc(e_pv, 1)

            scores(0)
            scores(1)
            for n in range(AN):
                turn(n)
                if n + 2 < AN:
                    scores(n + 2)
                if n % TB == TB - 1:
                    values(n // TB)

        def att_act(a):
            for x in range(5):
                if x == 0:
                    a.wait_ge(drained, end_of("att_kv"))
                else:
                    a.wait_ge(r_ms, x)
                a.activation(A_SQ, rope_src(x), ACT.Square).then_inc(r_sq, 1)
                a.wait_ge(r_ms, x + 1)
                if x:
                    a.wait_ge(r_qn, x)
                a.activation(A_RS, aux[:, 0, :], ACT.Ln, scale=1.0 / 64, bias=pc("eps")).then_inc(r_ln, 1)
                a.wait_ge(r_ln, x + 1)
                a.activation(A_RS, A_RS, ACT.Exp, scale=-0.5).then_inc(r_rs, 1)

            def copy_t(n):
                a.wait_ge(e_t, n + 1)
                if n % TB == 0 and n:
                    a.wait_ge(e_pv, n // TB)
                tb = n % TB
                a.activation(APT[:, :, tb * P:(tb + 1) * P], aux[:, 2, :].rearrange("p (s t) -> p s t", t=P),
                             ACT.Copy).then_inc(e_tc, 1)

            def out_hi(pr):
                a.wait_ge(e_pv, 2 * (pr + 1))
                a.activation(zh[:, 4 + pr, :], aux[:, 3, :], ACT.Copy).then_inc(z_hi, 1)

            for n in range(AN):
                a.wait_ge(e_max, n + 1)
                if n >= 2:
                    a.wait_ge(e_t, n - 1)
                a.activation(AP_[:, n % 2, :], aux[:, n % 2, :], ACT.Exp, bias=A_MAX[:, n:n + 1],
                             accum_out=A_SUM[:, n:n + 1]).then_inc(e_p, 1)
                if n:
                    copy_t(n - 1)
                if n % (2 * TB) == 1 and n > 1:
                    out_hi(n // (2 * TB) - 1)
            copy_t(AN - 1)
            out_hi(ATT_H // 2 - 1)

        def att_dve(v):
            v.wait_ge(rope_in, 16)
            for x in range(5):
                v.wait_ge(r_rs, x + 1)
                if x:
                    v.wait_ge(r_rot, x)
                v.scalar_tensor_tensor(A_QN, rope_src(x), pc("q_gain" if x < 4 else "k_gain"), A_RS,
                                       ALU.mult, ALU.mult).then_inc(r_qn, 1)
                v.wait_ge(r_qn, x + 1)
                if x:
                    v.wait_ge(r_out, x)
                by = 1.0 if x < 4 else SB_D ** -0.5
                v.scalar_tensor_tensor(A_T1, A_QN, by, ROPE[:, 0, :], ALU.mult, ALU.mult).then_inc(r_t1, 1)
                v.wait_ge(r_rot, x + 1)
                v.scalar_tensor_tensor(A_T2, aux[:, 1, :], by, ROPE[:, 1, :], ALU.mult, ALU.mult).then_inc(r_t2, 1)
                v.wait_ge(r_t1, x + 1)
                v.wait_ge(r_t2, x + 1)
                if x < 4:
                    v.tensor_tensor(AQ[:, x, :], A_T1, A_T2, ALU.add).then_inc(r_out, 1)
                else:
                    for kv in range(2):
                        for r in (0, 64):
                            ins = v.tensor_tensor(AKD[r:r + 64, kv, :], A_T1[kv * 64:kv * 64 + 64, :],
                                                  A_T2[kv * 64:kv * 64 + 64, :], ALU.add)
                    ins.then_inc(r_out, 1)

            def out_lo(pr):
                v.wait_ge(z_hi, 12 + pr + 1)
                v.tensor_tensor(zl[:, 4 + pr, :], aux[:, 3, :], zh[:, 4 + pr, :].bitcast(F), ALU.subtract
                                ).then_inc(z_lo, 1)

            def row_max(n):
                v.wait_ge(e_z, n + 1)
                v.tensor_reduce(A_MAX[:, n:n + 1], aux[:, n % 2, :], AX_X, ALU.max, negate=True).then_inc(e_max, 1)

            row_max(0)
            for n in range(AN):
                if n + 1 < AN:
                    row_max(n + 1)
                v.wait_ge(e_p, n + 1)
                v.reciprocal(A_RC[:, n:n + 1], A_SUM[:, n:n + 1]).then_inc(e_rc, 1)
                v.wait_ge(e_rc, n + 1)
                v.tensor_scalar(AP_[:, n % 2, :], AP_[:, n % 2, :], A_RC[:, n:n + 1], None, ALU.mult).then_inc(e_pn, 1)
                if n % (2 * TB) == 2 and n > 2:
                    out_lo(n // (2 * TB) - 1)
            out_lo(ATT_H // 2 - 1)

        MV = arena[:, 0:8, :].rearrange("p (b x) n -> p b (x n)", b=TB)
        MQK = arena[:, 8:16, :]
        CPAD = [arena[:, 16 + 2 * i:18 + 2 * i, :].rearrange("p a b -> p (a b)")[:, 0:T + 4] for i in range(4)]
        CO = arena[:, 24:28, :]
        m_zero, m_conv, m_raw, m_silu = sem("m_zero"), sem("m_conv"), sem("m_raw"), sem("m_silu")

        def conv5_dve(v):
            for i in range(4):
                ins = v.memset(CPAD[i][:, 0:2], 0.0)
                ins = v.memset(CPAD[i][:, T + 2:T + 4], 0.0)
            ins.then_inc(m_zero, 1)
            v.wait_ge(m_zero, 1)

            def body(c, slot, l):
                v.wait_ge(mm_done, c + 1)
                v.wait_ge(m_conv, l * 10)
                pads = arena[:, 16 + 4 * slot:20 + 4 * slot, :].rearrange("p (m a) b -> p m (a b)", m=2)
                v.tensor_scalar(pads[:, :, 2:T + 2], pairs[:, 2 * slot:2 * slot + 2, :], 1.0, None, ALU.mult
                                ).then_inc(drained, 1)
                v.wait_ge(drained, c + 1)
                for m in range(2):
                    pad = pads[:, m, :]
                    at = l * 2 + m
                    dst = CO[:, 2 * slot + m, :]
                    w = lambda tap: pc_at("od_conv_w", at + tap * 8)
                    v.tensor_scalar(dst, pad[:, 0:T], w(0), pc_at("od_conv_b", at), ALU.mult, ALU.add
                                    ).then_inc(m_conv, 1)
                    for tap in range(1, 5):
                        v.wait_ge(m_conv, l * 10 + (5 * m + tap))
                        out = dst if tap < 4 else MQK[:, bass.ds(at, 1), :]
                        src0, src1 = pad[:, tap:tap + T], dst
                        if tap == 4:
                            src0 = pads[:, m:m + 1, tap:tap + T]
                            src1 = CO[:, 2 * slot + m:2 * slot + m + 1, :]
                        v.scalar_tensor_tensor(out, src0, w(tap), src1, ALU.mult, ALU.add).then_inc(m_conv, 1)
            chunk_loop(v, "ml_qk", body)

        GROW = 40
        rows = {name: arena[0:64, 16 + i, :] for i, name in enumerate(("gi", "gf", "cap", "sum", "u", "mx", "m"))}
        ONE_ROWS = arena[0:64, 23, :]
        M_UT = small[:, 0:4 * GROW].rearrange("p (b c) -> p b c", c=GROW)
        m_gate, m_fc, m_fe, m_fl, m_lf = sem("m_gate"), sem("m_fc"), sem("m_fe"), sem("m_fl"), sem("m_lf")
        m_b, m_u, m_mx, m_m, m_ut, m_utc = sem("m_b"), sem("m_u"), sem("m_mx"), sem("m_m"), sem("m_ut"), sem("m_utc")

        m_em = sem("m_em")

        def gate_rows_dve(v):
            def body(c, slot, l):
                v.wait_ge(mm_done, c + 1)
                b = pairs[:, 2 * slot, :]
                v.tensor_scalar(rows["gi"][0:GROW, :], b[0:GROW, :], pc("gate_b", 0)[0:GROW], None, ALU.add
                                ).then_inc(m_gate, 1)
                v.tensor_scalar(rows["gf"][0:GROW, :], b[64:64 + GROW, :], pc("gate_b", 1)[64:64 + GROW], -1.0,
                                ALU.add, ALU.mult).then_inc(drained, 1)
            chunk_loop(v, "ml_g", body)

        def scans_dve(v):
            v.wait_ge(drained, end_of("ml_g"))
            r40 = lambda n: rows[n][0:GROW, :]
            v.memset(ONE_ROWS, 1.0).then_inc(m_zero, 1)
            v.tensor_scalar(r40("cap"), r40("gf"), SP_CAP, None, ALU.min).then_inc(m_fc, 1)
            v.wait_ge(m_fl, 1)
            v.tensor_tensor(r40("gf"), r40("gf"), r40("cap"), ALU.max).then_inc(m_lf, 1)
            v.wait_ge(m_lf, 1)
            v.wait_ge(m_zero, 2)
            v.memset(rows["sum"], 0.0).then_inc(m_b, 1)
            v.memset(rows["mx"], 0.0).then_inc(m_b, 1)
            v.wait_ge(m_b, 2)
            fwd, bwd = (slice(0, 8), slice(None)), (slice(32, 40), slice(None, None, -1))
            for d in (fwd, bwd):
                v.tensor_tensor_scan(rows["sum"][d], ONE_ROWS[d], rows["gf"][d], 0.0, ALU.mult, ALU.add
                                     ).then_inc(m_b, 1)
            v.wait_ge(m_b, 4)
            v.wait_ge(m_gate, 1)
            v.tensor_tensor(r40("u"), r40("gi"), r40("sum"), ALU.add).then_inc(m_u, 1)
            v.wait_ge(m_u, 1)
            for d in (fwd, bwd):
                v.tensor_tensor_scan(rows["mx"][d], rows["u"][d], rows["u"][d], 0.0, ALU.max, ALU.max
                                     ).then_inc(m_mx, 1)
            v.wait_ge(m_mx, 2)
            v.tensor_tensor(r40("m"), r40("mx"), r40("sum"), ALU.subtract).then_inc(m_m, 1)
            v.wait_ge(m_m, 1)
            v.tensor_scalar(r40("mx"), r40("mx"), -1.0, None, ALU.mult).then_inc(m_m, 1)
            v.tensor_scalar(r40("m"), r40("m"), -87.0, None, ALU.max).then_inc(m_m, 1)
            v.wait_ge(m_ut, 1)
            v.tensor_copy(M_UT, aux[:, 0, 0:4 * GROW].rearrange("p (b c) -> p b c", c=GROW)).then_inc(m_utc, 1)

        def scans_act(a):
            a.wait_ge(m_fc, 1)
            a.activation(rows["cap"][0:GROW, :], rows["cap"][0:GROW, :], ACT.Exp).then_inc(m_fe, 1)
            a.wait_ge(m_fe, 1)
            a.activation(rows["cap"][0:GROW, :], rows["cap"][0:GROW, :], ACT.Ln, bias=1.0).then_inc(m_fl, 1)
            a.wait_ge(m_m, 3)
            a.activation(rows["m"][0:GROW, :], rows["m"][0:GROW, :], ACT.Exp, scale=-1.0).then_inc(m_em, 1)

        def scans_pe(p):
            p.wait_ge(m_u, 1)
            for tb in range(TB):
                mm = p.transpose(aux[:, 0, tb * GROW:(tb + 1) * GROW], rows["u"][0:GROW, tb * P:(tb + 1) * P],
                                 cm("ident")[0:GROW, 0:GROW])
            mm.then_inc(m_ut, 1)

        ME = arena[:, 23:27, :]
        M_DG = arena[:, 18, :]
        M_MX = [arena[:, 27, :], ada_acc[:, :, :].rearrange("p a b -> p (a b)")]
        M_NUM, M_DEN = arena[:, 16:18, :], arena[:, 19:21, :]
        M_SQ, M_HS = arena[:, 23:25, :], arena[:, 25:27, :]

        def head_sum(hd):
            return MV[:, :, hd * P:(hd + 1) * P]

        def blocks(tile):
            return tile.rearrange("p (b c) -> p b c", c=P)

        k_bc, k_bcc, k_z, k_dg, k_e, k_s = (sem("k_bc"), sem("k_bcc"), sem("k_z"), sem("k_dg"), sem("k_e"),
                                            sem("k_s"))
        k_pv, k_num, k_den, k_em, k_dm = sem("k_pv"), sem("k_num"), sem("k_den"), sem("k_em"), sem("k_dm")
        k_ln, k_r, k_h, k_hs = sem("k_ln"), sem("k_r"), sem("k_h"), sem("k_hs")
        k_sq, k_ms, k_ml, k_mr, k_hn = sem("k_sq"), sem("k_ms"), sem("k_ml"), sem("k_mr"), sem("k_hn")

        def span(d, i):
            if d == 0:
                return (i * P, T), (i * P, (i + 1) * P), ((i + 1) * P, T)
            return (0, (i + 1) * P), (i * P, (i + 1) * P), (0, i * P)

        def ml_pe(p):
            def spread(name, hd, done):
                for d in range(2):
                    row = hd + 32 * d
                    mm = p.matmul(aux[:, 2 + d, :], cm("ident")[0:GROW, row:row + 1].to_broadcast([GROW, P]),
                                  rows[name][0:GROW, :], start=True, stop=True)
                mm.then_inc(done, 1)

            def score(g):
                hd, i = g // TB, g % TB
                r = (hd % 2) * 64
                if g >= 2:
                    p.wait_ge(k_s, 2 * (g - 1))
                p.matmul(aux[:, g % 2, :], MQK[r:r + 64, 4 + hd // 2, i * P:(i + 1) * P],
                         MQK[r:r + 64, hd // 2, :], start=True, stop=True).then_inc(k_z, 1)

            p.wait_ge(drained, end_of("ml_g"))
            p.wait_ge(m_utc, 1)
            p.wait_ge(m_silu, 1)
            p.wait_ge(m_m, 2)
            p.wait_ge(m_em, 1)
            spread("mx", 0, k_bc)
            score(0)
            score(1)
            for hd in range(ML_H + 1):
                for i in range(TB):
                    if hd < ML_H:
                        for d in range(2):
                            (lo, hi), _, _ = span(d, i)
                            if hd and i == 0:
                                p.wait_ge(k_num, hd)
                                p.wait_ge(k_den, hd)
                            p.wait_ge(k_s, 8 * hd + 2 * i + d + 1)
                            e = ME[:, 2 * d + i % 2, lo:hi]
                            p.matmul(pairs[:, d, lo:hi], MV[:, i, hd * P:(hd + 1) * P], e, start=(i == 0),
                                     stop=(i == TB - 1), skip_group_check=True)
                            p.matmul(pairs[:, 2 + d, lo:hi], cm("ones"), e, start=(i == 0), stop=(i == TB - 1),
                                     skip_group_check=True).then_inc(k_pv, 1)
                        if TB * hd + i + 2 < TB * ML_H:
                            score(TB * hd + i + 2)
                    if i == 0 and hd:
                        p.wait_ge(k_bcc, min(hd + 1, ML_H))
                        spread("m", hd - 1, k_em)
                    if i == 2 and hd + 1 < ML_H:
                        if hd:
                            p.wait_ge(k_dm, hd)
                        else:
                            p.wait_ge(k_bcc, 1)
                        spread("mx", hd + 1, k_bc)
            for hd in range(ML_H):
                p.wait_ge(k_sq, hd + 1)
                if hd >= 4:
                    p.wait_ge(k_ml, hd - 3)
                p.matmul(aux[:, hd % 4, :], cm("ones"), M_SQ[:, hd % 2, :], start=True, stop=True).then_inc(k_ms, 1)

        def ml_act(a):
            def copy_max(hd):
                a.wait_ge(k_bc, hd + 1)
                if hd:
                    a.wait_ge(k_e, 8 * hd)
                for d in range(2):
                    mm = a.activation(M_MX[d], aux[:, 2 + d, :], ACT.Copy)
                mm.then_inc(k_bcc, 1)

            copy_max(0)
            for hd in range(ML_H + 1):
                for i in range(TB):
                    for d in range(2 if hd < ML_H else 0):
                        _, (dlo, dhi), (lo, hi) = span(d, i)
                        step = 8 * hd + 2 * i + d
                        e = ME[:, 2 * d + i % 2, :]
                        a.wait_ge(k_bcc, hd + 1)
                        a.wait_ge(m_utc, 1)
                        if step >= 4:
                            a.wait_ge(k_pv, step - 3)
                        if hi > lo:
                            a.activation(e[:, lo:hi], M_MX[d][:, lo:hi], ACT.Exp,
                                         bias=M_UT[:, i, hd + 32 * d:hd + 32 * d + 1])
                        a.wait_ge(k_dg, step + 1)
                        a.activation(e[:, dlo:dhi], M_DG[:, (step % 4) * P:(step % 4 + 1) * P], ACT.Exp
                                     ).then_inc(k_e, 1)
                    if i == 0 and hd:
                        a.wait_ge(k_pv, 8 * hd)
                        if hd > 1:
                            a.wait_ge(k_hs, hd - 1)
                        a.activation(M_DEN, pairs[:, 2:4, :], ACT.Abs).then_inc(k_den, 1)
                        a.activation(M_NUM, pairs[:, 0:2, :], ACT.Copy).then_inc(k_num, 1)
                    if i == 2 and hd:
                        a.wait_ge(k_dm, hd)
                        a.activation(M_DEN, M_DEN, ACT.Ln).then_inc(k_ln, 1)
                        a.wait_ge(k_ln, hd)
                        a.activation(M_DEN, M_DEN, ACT.Exp, scale=-1.0).then_inc(k_r, 1)
                    if i == 3 and hd + 1 < ML_H:
                        copy_max(hd + 1)

            def square_head(hd):
                a.wait_ge(k_hs, hd + 1)
                if hd >= 2:
                    a.wait_ge(k_ms, hd - 1)
                a.activation(blocks(M_SQ[:, hd % 2, :]), head_sum(hd), ACT.Square).then_inc(k_sq, 1)

            square_head(0)
            square_head(1)
            for hd in range(ML_H):
                rs = M_HS[:, hd % 2, :]
                a.wait_ge(k_ms, hd + 1)
                if hd >= 2:
                    a.wait_ge(k_hn, hd - 1)
                a.activation(rs, aux[:, hd % 4, :], ACT.Ln, scale=1.0 / P, bias=pc("eps")).then_inc(k_ml, 1)
                a.wait_ge(k_ml, hd + 1)
                a.activation(rs, rs, ACT.Exp, scale=-0.5).then_inc(k_mr, 1)
                if hd + 2 < ML_H:
                    square_head(hd + 2)

        def ml_dve(v):
            for hd in range(ML_H + 1):
                for i in range(TB):
                    for d in range(2 if hd < ML_H else 0):
                        (lo, hi), (dlo, dhi), _ = span(d, i)
                        step = 8 * hd + 2 * i + d
                        v.wait_ge(k_bcc, hd + 1)
                        if step >= 4:
                            v.wait_ge(k_e, step - 3)
                        v.scalar_tensor_tensor(M_DG[:, (step % 4) * P:(step % 4 + 1) * P], M_MX[d][:, dlo:dhi],
                                               M_UT[:, i, hd + 32 * d:hd + 32 * d + 1],
                                               cm("neg_fwd" if d == 0 else "neg_bwd"), ALU.add, ALU.add
                                               ).then_inc(k_dg, 1)
                    for d in range(2 if hd < ML_H else 0):
                        (lo, hi), _, _ = span(d, i)
                        v.wait_ge(k_e, 8 * hd + 2 * i + d + 1)
                        v.wait_ge(k_z, TB * hd + i + 1)
                        e = ME[:, 2 * d + i % 2, lo:hi]
                        v.scalar_tensor_tensor(e, aux[:, i % 2, lo:hi], SB_D ** -0.5, e, ALU.mult, ALU.mult
                                               ).then_inc(k_s, 1)
                    if i == 1 and hd:
                        v.wait_ge(k_em, hd)
                        v.wait_ge(k_den, hd)
                        v.tensor_tensor(M_DEN, aux[:, 2:4, :], M_DEN, ALU.max).then_inc(k_dm, 1)
                    if i == 3 and hd:
                        v.wait_ge(k_r, hd)
                        v.wait_ge(k_num, hd)
                        v.tensor_tensor(M_NUM, M_NUM, M_DEN, ALU.mult).then_inc(k_h, 1)
                        v.wait_ge(k_h, hd)
                        v.tensor_tensor(head_sum(hd - 1), blocks(M_NUM[:, 0, :]), blocks(M_NUM[:, 1, :]), ALU.add
                                        ).then_inc(k_hs, 1)
            for hd in range(ML_H):
                v.wait_ge(k_mr, hd + 1)
                v.scalar_tensor_tensor(blocks(MQK[:, hd // 2 + 4 * (hd % 2), :]), head_sum(hd), pc("head_gain", hd),
                                       blocks(M_HS[:, hd % 2, :]), ALU.mult, ALU.mult).then_inc(k_hn, 1)

        OSIG = arena[:, 16:20, :]
        OV = arena[:, 20:24, :]
        o_sig, o_val = sem("o_sig"), sem("o_val")

        def ml_o_act(a):
            def body(c, slot, l):
                hi_part(a, c + 1, 1 - slot)
                a.wait_ge(mm_done, c + 1)
                a.activation(OSIG[:, 2 * slot:2 * slot + 2, :], pairs[:, 2 * slot:2 * slot + 2, :], ACT.Sigmoid
                             ).then_inc(o_sig, 1)
                a.wait_ge(o_val, l + 1)
                a.wait_ge(consts, 32)
                a.activation(zh[:, bass.ds(l * 2, 2), :], OV[:, 2 * slot:2 * slot + 2, :], ACT.Copy).then_inc(z_hi, 1)
            chunk_loop(a, "ml_o", body)

        def ml_o_dve(v):

            def body(c, slot, l):
                v.wait_ge(o_sig, l + 1)
                for m in range(2):
                    ins = v.tensor_tensor(OV[:, 2 * slot + m:2 * slot + m + 1, :], MQK[:, bass.ds(l + 4 * m, 1), :],
                                          OSIG[:, 2 * slot + m:2 * slot + m + 1, :], ALU.mult)
                ins.then_inc(o_val, 1)
                v.wait_ge(z_hi, l + (16 + 1))
                v.tensor_tensor(zl[:, bass.ds(l * 2, 2), :], OV[:, 2 * slot:2 * slot + 2, :],
                                zh[:, bass.ds(l * 2, 2), :].bitcast(F), ALU.subtract).then_inc(drained, 1)
            chunk_loop(v, "ml_o", body)

        block = ctx.enter_context(nc.Block())
        streams = {2048: w2048, 1024: w1024, HALF * P: w1408}

        def gate_col(layer, base):
            return lambda i: mod[:, layer, bass.ds(i + base, 1)]

        @block.sync
        def _(sp):
            sp.dma_start(par[:, :], par_d).then_inc(consts, 16)
            sp.dma_start(cst[:, :], cst_d).then_inc(consts, 16)
            for i in range(4):
                sp.dma_start(h[:, 2 * i:2 * i + 2, :], xT[:, 2 * i * T:(2 * i + 2) * T]
                             .rearrange("p (k t) -> p k t", t=T)).then_inc(x_in[i], 16)
            for stage, kind, _ in STAGES:
                w = WIDTH[kind]
                if stage == "g_q":
                    sp.wait_ge(drained, end_of("sb_q"))
                    sp.dma_start(G_CST[:, 0:GLA_W], gla_d).then_inc(gla_in, 16)
                def body(c, slot, l):
                    if not (is_static(c) and c < 2):
                        sp.wait_ge(lo_done, c - 1)
                    sp.dma_start(raw[:, slot, 0:w], streams[w][bass.ds(l + ROW0[stage], 1), :, :]
                                 .rearrange("a p n -> p (a n)")).then_inc(raw_full[slot], 16)
                    if stage in ADA_OF:
                        ada_load(sp, l + ADA_OF[stage], ada_slot(stage, slot))
                if stage not in ("out", "att_out"):
                    chunk_loop(sp, stage, body)
                else:
                    chunk_loop(sp, stage, body, hi=2)
                    layer = 0 if stage == "out" else 1
                    if layer == 0:
                        sp.wait_ge(drained, end_of("branch"))
                    else:
                        sp.wait_ge(z_lo, 16)
                    for A in (ADA_N * layer, ADA_N * layer + 1):
                        ada_load(sp, A, A % 2)
                    chunk_loop(sp, stage, body, lo=2)
            for k in range(KT):
                sp.wait_ge(drained, C0["o_down1"] + k + 1)
                sp.dma_start(outT[:, k * T:(k + 1) * T], h[:, k, :]).then_inc(stored, 16)
            sp.wait_ge(stored, 16 * KT)

        @block.gpsimd
        def _(g):
            for stage, kind, _ in STAGES:
                w = WIDTH[kind]

                def body(c, slot, l):
                    g.wait_ge(hi_done, c + 1)
                    g.tensor_tensor(wl[:, slot, 0:w], raw[:, slot, 0:w], wh[:, slot, 0:w].bitcast(F), ALU.subtract
                                    ).then_inc(lo_done, 1)
                chunk_loop(g, stage, body)

        @block.scalar
        def _(a):
            a.wait_ge(consts, 32)
            a.activation(cond[:, :], pc("c", 0, KT), ACT.Silu).then_inc(s("cond_done"), 1)
            norm_act(a, "n_mix")
            for stage in ("sb_q", "sb_k", "sb_v"):
                hi_only(a, stage)
            sb_act(a)
            for stage in ("g_q", "g_k", "g_v", "g_r", "g_a"):
                hi_only(a, stage)
            gla_act(a)
            gates_act(a)
            branch_act(a)
            hi_only(a, "out")
            norm_act(a, "n_ffn")
            for i in range(2):
                up_act(a, f"up{i}")
                hi_only(a, f"down{i}")
            a.wait_ge(drained, end_of("up1"))
            a.dma_start(ROPE[:, :, :], rope_d.rearrange("p (a t) -> p a t", t=T)).then_inc(rope_in, 16)
            a.dma_start(POOLC[:, :, :], pool_d.rearrange("p (a t) -> p a t", t=T)).then_inc(pool_in, 16)
            norm_act(a, "n_final")
            norm_act(a, "n_e1")
            for stage in ("pool_u", "att_q", "att_kv"):
                hi_only(a, stage)
            pool_out_act(a)
            att_act(a)
            hi_only(a, "att_out")
            norm_act(a, "n_e2")
            for i in range(2):
                up_act(a, f"e_up{i}")
                hi_only(a, f"e_down{i}")
            norm_act(a, "n_o1")
            hi_only(a, "ml_qk")
            a.wait_ge(m_conv, 40)
            a.activation(MQK, MQK, ACT.Silu).then_inc(m_silu, 1)
            for stage in ("ml_v", "ml_g"):
                hi_only(a, stage)
            a.preload_act_table_set("natural_log_exp_and_others")
            scans_act(a)
            ml_act(a)
            ml_o_act(a)
            hi_only(a, "ml_out")
            norm_act(a, "n_o2")
            for i in range(2):
                up_act(a, f"o_up{i}")
                hi_only(a, f"o_down{i}")

        @block.vector
        def _(v):
            norm_dve(v, "n_mix")
            drain_copy(v, "sb_q", lambda l: SBQ[:, bass.ds(l * 2, 2), :], SB_D ** -0.5)
            drain_copy(v, "sb_k", lambda l: SBK[:, bass.ds(l * 2, 2), :])
            drain_copy(v, "sb_v", lambda l: SBV[:, :, bass.ds(l * 256, 256)])
            sb_dve(v)
            drain_copy(v, "g_q", lambda l: GQ, SB_D ** -0.5)
            drain_copy(v, "g_k", lambda l: GK)
            drain_copy(v, "g_v", lambda l: GV[:, :, bass.ds(l * 256, 256)])
            drain_copy(v, "g_r", lambda l: GR[:, bass.ds(l * 2, 2), :])

            def low_rank(c, slot, l):
                v.wait_ge(mm_done, c + 1)
                v.tensor_copy(G_A[0:16, :], pairs[0:16, 2 * slot, :]).then_inc(drained, 1)
            chunk_loop(v, "g_a", low_rank)
            gla_dve(v)
            gates_dve(v)
            branch_dve(v)
            v.wait_ge(s("cond_done"), 1)
            for A in range(2):
                ada_dve(v, A, A)
            drain_residual(v, "out")
            norm_dve(v, "n_ffn")
            for i in range(2):
                ins = v.memset(apad[i][:, 0:2], 0.0)
            ins.then_inc(s("pad_zero"), 1)
            v.wait_ge(s("pad_zero"), 1)
            for i in range(2):
                up_dve(v, f"up{i}")
                if i == 1:
                    mod_dve(v, 0)
                drain_residual(v, f"down{i}")
            norm_dve(v, "n_final")
            v.wait_ge(mod_done, 2)
            norm_dve(v, "n_e1")
            v.wait_ge(x_ready, KT * 3)
            v.memset(UP[:, :, 0:PAD], 0.0)
            v.memset(UP[:, :, PAD + T:UW], 0.0).then_inc(u_zero, 1)
            v.wait_ge(u_zero, 1)
            drain_copy(v, "pool_u", lambda l: UP[:, bass.ds(l * 2, 2), PAD:PAD + T])
            v.wait_ge(drained, end_of("pool_u"))
            pool_dve(v)
            drain_copy(v, "att_q", lambda l: AQ[:, bass.ds(l * 2, 2), :])

            def kv(c, slot, l):
                v.wait_ge(mm_done, c + 1)
                v.tensor_copy(AK, pairs[:, 2 * slot, :])
                v.tensor_copy(AV, pairs[:, 2 * slot + 1, :].rearrange("p (b n) -> p b n", n=P)).then_inc(drained, 1)
            chunk_loop(v, "att_kv", kv)
            pool_out_dve(v)
            att_dve(v)
            for A in (ADA_N, ADA_N + 1):
                ada_dve(v, A, A % 2)
            drain_residual(v, "att_out", gate_col(0, 16))
            norm_dve(v, "n_e2")
            for i in range(2):
                up_dve(v, f"e_up{i}")
                if i == 1:
                    mod_dve(v, 1)
                drain_residual(v, f"e_down{i}", gate_col(0, 40))
            v.wait_ge(mod_done, 4)
            norm_dve(v, "n_o1")
            conv5_dve(v)
            drain_copy(v, "ml_v", lambda l: MV[:, :, bass.ds(l * 256, 256)])
            gate_rows_dve(v)
            scans_dve(v)
            ml_dve(v)
            ml_o_dve(v)
            drain_residual(v, "ml_out", gate_col(1, 16))
            norm_dve(v, "n_o2")
            for i in range(2):
                up_dve(v, f"o_up{i}")
                drain_residual(v, f"o_down{i}", gate_col(1, 40))

        @block.tensor
        def _(p):
            norm_pe(p, "n_mix")
            linear_pe(p, "sb_q", norm=0)
            linear_pe(p, "sb_k")
            linear_pe(p, "sb_v")
            sb_pe(p)
            for stage in ("g_q", "g_k", "g_v", "g_r", "g_a"):
                linear_pe(p, stage)
            gla_pe(p)
            linear_pe(p, "gates")
            linear_pe(p, "branch", (z_lo, 8))
            linear_pe(p, "out", (drained, end_of("branch")))
            ada_pe(p, 0, 0, 0)
            norm_pe(p, "n_ffn")
            for i in range(2):
                linear_pe(p, f"up{i}", norm=1 if i == 0 else None)
                if i == 1:
                    ada_pe(p, ADA_N - 1, (ADA_N - 1) % 2, 0)
                linear_pe(p, f"down{i}", (drained, end_of(f"up{i}")))
            norm_pe(p, "n_final")
            norm_pe(p, "n_e1")
            linear_pe(p, "pool_u", norm=2)
            linear_pe(p, "att_q")
            linear_pe(p, "att_kv")
            pool_pe(p)
            att_pe(p)
            linear_pe(p, "att_out", (z_lo, 16))
            ada_pe(p, ADA_N, 0, 1)
            norm_pe(p, "n_e2")
            for i in range(2):
                linear_pe(p, f"e_up{i}", norm=3 if i == 0 else None)
                if i == 1:
                    ada_pe(p, 2 * ADA_N - 1, 1, 1)
                linear_pe(p, f"e_down{i}", (drained, end_of(f"e_up{i}")))
            norm_pe(p, "n_o1")
            linear_pe(p, "ml_qk", norm=4)
            linear_pe(p, "ml_v")
            linear_pe(p, "ml_g")
            scans_pe(p)
            ml_pe(p)
            p.wait_ge(k_num, ML_H)
            p.wait_ge(k_den, ML_H)
            linear_pe(p, "ml_o")
            linear_pe(p, "ml_out", (drained, end_of("ml_o")))
            norm_pe(p, "n_o2")
            for i in range(2):
                linear_pe(p, f"o_up{i}", norm=5 if i == 0 else None)
                linear_pe(p, f"o_down{i}", (drained, end_of(f"o_up{i}")))


def chunks_of(w, cols):
    k, n = w.shape
    return np.ascontiguousarray(w.reshape(k // P, P, n // cols, cols).transpose(2, 1, 0, 3)).reshape(
        n // cols, P, k // P * cols)


def constant_matrices():
    r = np.arange(P)
    s_, t_ = r[:, None], r[None, :]
    rot = np.zeros((P, P), np.float32)
    rot[r[1::2], r[0::2]] = -1.0
    rot[r[0::2], r[1::2]] = 1.0
    mats = {
        "ident": s_ == t_, "ntri": -1.0 * (s_ >= t_), "ones": np.ones((P, P)), "nones": -np.ones((P, P)),
        "neg_strict": NEG * (s_ >= t_), "keep_strict": s_ < t_,
        "gla_mask": (s_ <= t_) & (s_ // GLA_C == t_ // GLA_C), "bd64": s_ // 64 == t_ // 64, "rot": rot,
        "neg_fwd": NEG * (s_ > t_), "neg_bwd": NEG * (s_ < t_),
    }
    return np.concatenate([np.asarray(mats[n], np.float32) for n in CST_COLS], axis=1)


def rope_tables():
    t = np.arange(T)
    inv = np.float32(10000.0) ** (-np.arange(16, dtype=np.float32) / np.float32(16))
    ang = np.concatenate([(t // 64).astype(np.float32)[:, None] * inv, (t % 64).astype(np.float32)[:, None] * inv],
                         axis=1)
    rows = [np.tile(np.repeat(f(ang).T, 2, axis=0), (2, 1)) for f in (np.cos, np.sin)]
    return np.concatenate(rows, axis=1).astype(np.float32)


def pool_reciprocals():
    t = np.arange(T)
    rows = []
    for w in (2, 4, 8, 16):
        lo, hi = np.clip(t - w // 2, 0, T), np.clip(t + w - w // 2, 0, T)
        rows.append(np.float32(1.0) / (hi - lo).astype(np.float32))
    return np.broadcast_to(np.concatenate(rows)[None], (P, 4 * T)).astype(np.float32)


def lay_out(i):
    f32 = np.float32
    w_in = i["w_in"][0]
    at = np.cumsum([0, 512, 512, 512, 256, 256, 512, 512, 16, 1024, 1024])
    cut = lambda n: w_in[:, at[n]:at[n + 1]]

    def pad_cols(w, places):
        out = np.zeros((w.shape[0], P), f32)
        for (a, b), place in places:
            out[:, place:place + b - a] = w[:, a:b]
        return out

    def paired(a, g):
        k = a.shape[0]
        return np.concatenate([a.reshape(k, -1, 1, P), g.reshape(k, -1, 1, P)], axis=2).reshape(k, -1)

    od = i["od_w_in_2"][0]
    ev = i["ev_w_in_2"][0]
    gate_places = [((0, 8), 0), ((16, 24), 32), ((8, 16), 64), ((24, 32), 96)]
    half = HALF * P
    s = {
        "sb_q": cut(0), "sb_k": cut(1), "sb_v": cut(2), "g_q": cut(3), "g_k": cut(4), "g_v": cut(5), "g_r": cut(6),
        "g_a": pad_cols(cut(7), [((0, 16), 0)]), "gates": w_in[:, at[8]:at[10]],
        "branch": np.concatenate([i["w_branch_sb"][0], i["w_branch_gla"][0]]), "out": i["w_out"][0],
        "pool_u": ev[:, 0:512], "att_q": ev[:, 512:1024], "att_kv": ev[:, 1024:1280], "att_out": i["ev_w_out_2"][0],
        "ml_qk": od[:, 0:1024], "ml_v": od[:, 1024:2048], "ml_o": od[:, 2048:3072],
        "ml_g": pad_cols(od[:, 3072:3104], gate_places), "ml_out": i["od_w_out_2"][0],
    }
    ffns = (("", i["w_ffn_in"][0][:, :FF], i["w_ffn_in"][0][:, FF:], i["w_ffn_out"][0]),
            ("e_", i["ffn_w1_2"][0], i["ffn_w3_2"][0], i["ffn_w2_2"][0]),
            ("o_", i["ffn_w1_2"][1], i["ffn_w3_2"][1], i["ffn_w2_2"][1]))
    for pre, wa, wg, wo in ffns:
        for n in range(2):
            c = slice(n * half, (n + 1) * half)
            s[f"{pre}up{n}"] = paired(wa[:, c], wg[:, c])
            s[f"{pre}down{n}"] = wo[c]
    streams = {}
    for name, kind, count in STAGES:
        ch = chunks_of(s[name], 256 if WIDTH[kind] == 2048 else P)
        streams.setdefault(WIDTH[kind], []).append(ch)
    col = lambda v: np.asarray(v, f32).reshape(-1, P).T
    gate_b = np.zeros((P, 2), f32)
    gb = i["od_gate_b_2"][0]
    for (a, b), place in gate_places:
        gate_b[place:place + b - a, place // 64] = gb[a:b]
    par = {
        "norm_mix": col(i["norm_mix_g"][0]), "b_gate": col(i["b_gate"][0]), "b_alpha": col(i["b_alpha"][0]),
        "gla_g": col(i["gla_norm_g"][0]), "norm_ffn": col(i["norm_ffn_g"][0]), "conv_w": col(i["conv_w"][0]),
        "conv_b": col(i["conv_b"][0]), "norm_final": col(i["norm_final_g"]), "c": col(i["c_2"][0]),
        "ada_b": col(i["ada_b_2"]), "b_pool": col(i["ev_b_pool_2"][0]), "pool_scale": col(i["ev_pool_scale_2"][0]),
        "q_gain": np.tile(i["ev_q_gain_2"][0], 2)[:, None], "k_gain": np.tile(i["ev_k_gain_2"][0], 2)[:, None],
        "od_conv_w": col(i["od_conv_w_2"][0]), "od_conv_b": col(i["od_conv_b_2"][0]), "gate_b": gate_b,
        "head_gain": col(i["od_head_gain_2"][0]), "eps": np.full((P, 1), EPS, f32),
    }
    reset = np.broadcast_to((np.arange(T) % GLA_C != 0).astype(f32)[None], (P, T))
    alpha = np.zeros((P, 256), f32)
    alpha[0:16] = i["w_alpha_up"][0]
    w_pool = i["ev_w_pool_2"][0].transpose(1, 0, 2).reshape(P, 4 * P)
    cat = lambda xs: np.ascontiguousarray(np.concatenate(xs, axis=1), dtype=f32)
    arrays = {
        "xT": np.ascontiguousarray(i["x"][0].T.reshape(KT, P, T).transpose(1, 0, 2)).reshape(P, KT * T),
        "w2048": np.concatenate(streams[2048]), "w1024": np.concatenate(streams[1024]),
        "w1408": np.concatenate(streams[HALF * P]),
        "ada": np.concatenate([chunks_of(i["ada_w_2"][n], 256) for n in range(2)]),
        "par": cat([par[n] for n in PAR_COLS]), "cst": constant_matrices(), "gla": cat([reset, alpha]),
        "rope": rope_tables(), "pool": cat([pool_reciprocals(), w_pool]),
    }
    return {f"in_{name}": a for name, a in arrays.items()}


def kernel(**inputs):
    import concourse.bacc as bacc
    from concourse.bass_utils import run_bass_kernel_spmd

    nc = bacc.Bacc("TRN2", target_bir_lowering=False, num_devices=1)
    arrays = lay_out({k: np.asarray(v) for k, v in inputs.items()})
    aps = [nc.dram_tensor(n, a.shape, F, kind="ExternalInput").ap() for n, a in arrays.items()]
    out = nc.dram_tensor("outT", (P, KT * T), F, kind="ExternalOutput").ap()
    build(nc, *aps, out)
    r = run_bass_kernel_spmd(nc, [arrays], core_ids=[0])
    got = r.results[0]["outT"]
    return np.ascontiguousarray(got.reshape(P, KT, T).transpose(2, 1, 0)).reshape(1, T, D)
```
